# Optimizing a Trainium2 kernel written in Bass

```python
import math
import jax
import jax.numpy as jnp
from jax import lax
import numpy as np
import jax, jax.numpy as jnp

D_MODEL = 1024
BATCH = 1
SEQ = 512
DEPTH = 2

N_MIXERS = 2
N_POOL_LAYERS = (DEPTH + 1) // 2
N_ATTN_LAYERS = DEPTH // 2

POOL_WINDOWS = (2, 4, 8, 16)
N_POOL_GROUPS = len(POOL_WINDOWS)
POOL_GC = D_MODEL // N_POOL_GROUPS

HEAD_DIM = 64
N_HEADS = D_MODEL // HEAD_DIM
N_KV_HEADS = 4
N_GROUPS = N_HEADS // N_KV_HEADS
WINDOW = 128
BLOCK = 128
QKV_DIM = (N_HEADS + 2 * N_KV_HEADS) * HEAD_DIM

D_FF = 2816
CONV_W = 3

RMS_EPS = 1e-6


def rms_norm(x, g):
    xf = x.astype(jnp.float32)
    y = xf * lax.rsqrt(jnp.mean(xf * xf, axis=-1, keepdims=True) + RMS_EPS)
    return (y * g.astype(jnp.float32)).astype(x.dtype)

def alibi_slopes(n_heads):
    h = jnp.arange(1, n_heads + 1, dtype=jnp.float32)
    return jnp.exp2(-8.0 / n_heads * h)

def pool_mixer(h, w, b, scale):
    B, S, D = h.shape
    hf = h.astype(jnp.float32)
    csum = jnp.cumsum(hf, axis=1)
    t1 = jnp.arange(1, S + 1)
    outs = []
    for gi, win in enumerate(POOL_WINDOWS):
        sl = slice(gi * POOL_GC, (gi + 1) * POOL_GC)
        c = csum[..., sl]
        lo = jnp.pad(c, ((0, 0), (win, 0), (0, 0)))[:, :S]
        count = jnp.minimum(t1, win).astype(jnp.float32)
        mean = (c - lo) / count[None, :, None]
        outs.append(mean - hf[..., sl])
    p = jnp.stack(outs, axis=2).astype(h.dtype)
    y = jnp.einsum('bsgc,gcd->bsgd', p, w) + b
    return y.reshape(B, S, D) * scale

def swa_sink_attention(h, w_qkv, b_qkv, sinks, w_o):
    B, S, _ = h.shape
    nb = S // BLOCK
    qkv = h @ w_qkv + b_qkv
    q = qkv[..., :N_HEADS * HEAD_DIM].reshape(B, nb, BLOCK, N_KV_HEADS, N_GROUPS, HEAD_DIM)
    k = qkv[..., N_HEADS * HEAD_DIM:(N_HEADS + N_KV_HEADS) * HEAD_DIM].reshape(B, S, N_KV_HEADS, HEAD_DIM)
    v = qkv[..., (N_HEADS + N_KV_HEADS) * HEAD_DIM:].reshape(B, S, N_KV_HEADS, HEAD_DIM)

    def band(t):
        tp = jnp.pad(t, ((0, 0), (BLOCK, 0), (0, 0), (0, 0)))[:, :S]
        prev = tp.reshape(B, nb, BLOCK, N_KV_HEADS, HEAD_DIM)
        cur = t.reshape(B, nb, BLOCK, N_KV_HEADS, HEAD_DIM)
        return jnp.concatenate([prev, cur], axis=2)

    kb, vb = band(k), band(v)
    scores = jnp.einsum('bnqkgd,bnskd->bnkgqs', q, kb).astype(jnp.float32) * (HEAD_DIM ** -0.5)

    qi = jnp.arange(BLOCK)[:, None]
    kj = jnp.arange(2 * BLOCK)[None, :]
    dist = qi + BLOCK - kj
    key_pos = jnp.arange(nb)[:, None] * BLOCK - BLOCK + jnp.arange(2 * BLOCK)[None, :]
    mask = ((dist >= 0) & (dist < WINDOW))[None] & (key_pos >= 0)[:, None, :]

    slopes = alibi_slopes(N_HEADS).reshape(N_KV_HEADS, N_GROUPS)
    bias = -slopes[:, :, None, None] * dist.astype(jnp.float32)[None, None]
    scores = jnp.where(mask[None, :, None, None], scores + bias, -jnp.inf)

    sink = sinks.astype(jnp.float32).reshape(N_KV_HEADS, N_GROUPS)[None, None, :, :, None, None]
    m = jnp.maximum(jnp.max(scores, axis=-1, keepdims=True), sink)
    p = jnp.exp(scores - m)
    denom = jnp.sum(p, axis=-1, keepdims=True) + jnp.exp(sink - m)
    probs = (p / denom).astype(v.dtype)
    o = jnp.einsum('bnkgqs,bnskd->bnqkgd', probs, vb).reshape(B, S, N_HEADS * HEAD_DIM)
    return o @ w_o

def conv_glu_ffn(h, w_in, conv_w, conv_b, w_out):
    u = h @ w_in
    c = lax.conv_general_dilated(
        u, conv_w[:, None, :].astype(u.dtype), window_strides=(1,),
        padding=[(CONV_W - 1, 0)], dimension_numbers=('NWC', 'WIO', 'NWC'),
        feature_group_count=2 * D_FF) + conv_b
    a, g = c[..., :D_FF], c[..., D_FF:]
    return (a * jax.nn.silu(g)) @ w_out

def first_inputs(seed: int = 0) -> dict:
    key = jax.random.key(seed)
    ks = jax.random.split(key, 16)
    f32 = jnp.float32
    nrm = lambda k, shape, s: jax.random.normal(k, shape, f32) * s
    return {
        "x": nrm(ks[0], (BATCH, SEQ, D_MODEL), 1.0),
        "pool_w": nrm(ks[1], (N_POOL_LAYERS, N_POOL_GROUPS, POOL_GC, POOL_GC), POOL_GC ** -0.5),
        "pool_b": nrm(ks[2], (N_POOL_LAYERS, N_POOL_GROUPS, POOL_GC), 0.02),
        "pool_scale": 1.0 + nrm(ks[3], (N_POOL_LAYERS, D_MODEL), 0.05),
        "attn_w_qkv": nrm(ks[4], (N_ATTN_LAYERS, D_MODEL, QKV_DIM), D_MODEL ** -0.5),
        "attn_b_qkv": nrm(ks[5], (N_ATTN_LAYERS, QKV_DIM), 0.02),
        "attn_sinks": nrm(ks[6], (N_ATTN_LAYERS, N_HEADS), 0.5),
        "attn_w_o": nrm(ks[7], (N_ATTN_LAYERS, N_HEADS * HEAD_DIM, D_MODEL), (N_HEADS * HEAD_DIM) ** -0.5),
        "norm_mix": 1.0 + nrm(ks[8], (DEPTH, D_MODEL), 0.05),
        "norm_ffn": 1.0 + nrm(ks[9], (DEPTH, D_MODEL), 0.05),
        "ffn_w_in": nrm(ks[10], (DEPTH, D_MODEL, 2 * D_FF), D_MODEL ** -0.5),
        "ffn_conv_w": nrm(ks[11], (DEPTH, CONV_W, 2 * D_FF), CONV_W ** -0.5),
        "ffn_conv_b": nrm(ks[12], (DEPTH, 2 * D_FF), 0.02),
        "ffn_w_out": nrm(ks[13], (DEPTH, D_FF, D_MODEL), D_FF ** -0.5),
        "norm_f": 1.0 + nrm(ks[14], (D_MODEL,), 0.05),
    }

def first_block(x, pool_w, pool_b, pool_scale, attn_w_qkv, attn_b_qkv, attn_sinks, attn_w_o,
              norm_mix, norm_ffn, ffn_w_in, ffn_conv_w, ffn_conv_b, ffn_w_out, norm_f):
    h = x
    for i in range(DEPTH):
        hn = rms_norm(h, norm_mix[i])
        j = i // N_MIXERS
        if i % N_MIXERS == 0:
            mix = pool_mixer(hn, pool_w[j], pool_b[j], pool_scale[j])
        else:
            mix = swa_sink_attention(hn, attn_w_qkv[j], attn_b_qkv[j], attn_sinks[j], attn_w_o[j])
        h = h + mix
        hn = rms_norm(h, norm_ffn[i])
        h = h + conv_glu_ffn(hn, ffn_w_in[i], ffn_conv_w[i], ffn_conv_b[i], ffn_w_out[i])
    return rms_norm(h, norm_f)


DEPTH_2 = 1

N_MIXERS_2 = 4
D_FF_2 = 4 * D_MODEL
CONV_KERNEL = 31
SHORT_CONV = 3
FOX_HEADS = 16
FOX_HEAD_DIM = D_MODEL // FOX_HEADS
Q_BLOCK = 128
GLA_HEADS = 4
GLA_DK = D_MODEL // 2
GLA_DV = D_MODEL
GLA_DK_HEAD = GLA_DK // GLA_HEADS
GLA_DV_HEAD = GLA_DV // GLA_HEADS
GLA_GATE_RANK = 16
GLA_TAU = 16.0
GLA_CHUNK = 64


def _layers_of(m):
    return len(range(m, DEPTH_2, N_MIXERS_2))

def rms_norm_2(x, g):
    x32 = x.astype(jnp.float32)
    y = x32 * lax.rsqrt(jnp.mean(x32 * x32, axis=-1, keepdims=True) + RMS_EPS)
    return (y * g.astype(jnp.float32)).astype(x.dtype)

def layer_norm(x, g, b):
    x32 = x.astype(jnp.float32)
    mu = jnp.mean(x32, axis=-1, keepdims=True)
    xc = x32 - mu
    y = xc * lax.rsqrt(jnp.mean(xc * xc, axis=-1, keepdims=True) + RMS_EPS)
    return (y * g.astype(jnp.float32) + b.astype(jnp.float32)).astype(x.dtype)

def conformer_conv(x, w_in, b_in, conv_w, conv_b, ln_g, ln_b, w_out, b_out):
    a, g = jnp.split(x @ w_in + b_in, 2, axis=-1)
    h = a * jax.nn.sigmoid(g)
    h = lax.conv_general_dilated(
        h, conv_w[:, None, :].astype(h.dtype), window_strides=(1,),
        padding=[(CONV_KERNEL - 1, 0)],
        dimension_numbers=("NWC", "WIO", "NWC"),
        feature_group_count=D_MODEL) + conv_b
    h = jax.nn.silu(layer_norm(h, ln_g, ln_b))
    return h @ w_out + b_out

def short_gated_conv(x, w_in, conv_w, w_out):
    S = x.shape[1]
    gate_b, gate_c, h = jnp.split(x @ w_in, 3, axis=-1)
    u = gate_c * h
    up = jnp.pad(u, ((0, 0), (SHORT_CONV - 1, 0), (0, 0)))
    conv = conv_w[0] * up[:, 0:S]
    for k in range(1, SHORT_CONV):
        conv = conv + conv_w[k] * up[:, k:k + S]
    return (gate_b * conv) @ w_out

def forgetting_attention(x, w_qkv, q_g, k_g, w_f, b_f, w_out):
    Bsz, S, _ = x.shape
    q, k, v = jnp.split(x @ w_qkv, 3, axis=-1)
    heads = lambda t: t.reshape(Bsz, S, FOX_HEADS, FOX_HEAD_DIM).transpose(0, 2, 1, 3)
    q = rms_norm_2(heads(q), q_g)
    k = rms_norm_2(heads(k), k_g)
    v = heads(v)
    log_f = jax.nn.log_sigmoid((x @ w_f + b_f).astype(jnp.float32))
    c = jnp.cumsum(log_f, axis=1).transpose(0, 2, 1)
    n_blk = S // Q_BLOCK
    qb = q.reshape(Bsz, FOX_HEADS, n_blk, Q_BLOCK, FOX_HEAD_DIM).transpose(2, 0, 1, 3, 4)
    cb = c.reshape(Bsz, FOX_HEADS, n_blk, Q_BLOCK).transpose(2, 0, 1, 3)
    starts = jnp.arange(n_blk, dtype=jnp.int32) * Q_BLOCK
    key_pos = jnp.arange(S, dtype=jnp.int32)
    scale = FOX_HEAD_DIM ** -0.5

    def block(args):
        q_i, c_i, start = args
        s = jnp.einsum("bhqd,bhkd->bhqk", q_i, k).astype(jnp.float32) * scale
        s = s + c_i[..., :, None] - c[:, :, None, :]
        q_pos = start + jnp.arange(Q_BLOCK, dtype=jnp.int32)
        s = jnp.where(key_pos[None, :] <= q_pos[:, None], s, -jnp.inf)
        p = jax.nn.softmax(s, axis=-1)
        return jnp.einsum("bhqk,bhkd->bhqd", p.astype(v.dtype), v)

    o = lax.map(block, (qb, cb, starts))
    o = o.transpose(1, 0, 3, 2, 4).reshape(Bsz, S, D_MODEL)
    return o @ w_out

def gated_linear_attention(x, w_in, w_g1, w_g2, b_g, o_g, w_out):
    Bsz, S, _ = x.shape
    q, k, v, r = jnp.split(x @ w_in, [GLA_DK, 2 * GLA_DK, 2 * GLA_DK + GLA_DV], axis=-1)
    log_a = jax.nn.log_sigmoid(((x @ w_g1) @ w_g2 + b_g).astype(jnp.float32)) / GLA_TAU
    nc = S // GLA_CHUNK

    def chunks(t, dh):
        return t.astype(jnp.float32).reshape(Bsz, nc, GLA_CHUNK, GLA_HEADS, dh).transpose(1, 0, 3, 2, 4)

    qc = chunks(q, GLA_DK_HEAD) * (GLA_DK_HEAD ** -0.5)
    kc = chunks(k, GLA_DK_HEAD)
    vc = chunks(v, GLA_DV_HEAD)
    b = jnp.cumsum(chunks(log_a, GLA_DK_HEAD), axis=-2)
    b_last = b[..., -1:, :]
    q_t = qc * jnp.exp(b)
    k_t = kc * jnp.exp(-b)
    k_dec = kc * jnp.exp(b_last - b)
    causal = jnp.tril(jnp.ones((GLA_CHUNK, GLA_CHUNK), dtype=bool))
    att = jnp.where(causal, jnp.einsum("nbhtd,nbhsd->nbhts", q_t, k_t), 0.0)
    o_intra = jnp.einsum("nbhts,nbhse->nbhte", att, vc)

    def step(state, inp):
        q_i, kd_i, v_i, dl_i = inp
        o_i = jnp.einsum("bhtd,bhde->bhte", q_i, state)
        state = state * jnp.exp(dl_i)[..., None] + jnp.einsum("bhsd,bhse->bhde", kd_i, v_i)
        return state, o_i

    s0 = jnp.zeros((Bsz, GLA_HEADS, GLA_DK_HEAD, GLA_DV_HEAD), jnp.float32)
    _, o_inter = lax.scan(step, s0, (q_t, k_dec, vc, b_last[..., 0, :]))
    o = rms_norm_2(o_intra + o_inter, o_g)
    o = o.transpose(1, 0, 3, 2, 4).reshape(Bsz, S, GLA_DV).astype(x.dtype)
    return (o * jax.nn.silu(r)) @ w_out

def squared_relu_mlp(x, w1, w2):
    return jnp.square(jax.nn.relu(x @ w1)) @ w2

def second_inputs(seed: int = 0) -> dict:
    key = jax.random.key(seed)
    ks = iter(jax.random.split(key, 40))
    f32 = jnp.float32

    def nrm(shape, scale):
        return jax.random.normal(next(ks), shape, f32) * scale

    def gain(shape):
        return 1.0 + nrm(shape, 0.05)

    nA, nB, nC, nD = (_layers_of(m) for m in range(N_MIXERS_2))
    D = D_MODEL
    return {
        "x": nrm((BATCH, SEQ, D), 1.0),
        "mix_norm": gain((DEPTH_2, D)),
        "mlp_norm": gain((DEPTH_2, D)),
        "mlp_w1": nrm((DEPTH_2, D, D_FF_2), D ** -0.5),
        "mlp_w2": nrm((DEPTH_2, D_FF_2, D), D_FF_2 ** -0.5),
        "a_w_in": nrm((nA, D, 2 * D), D ** -0.5),
        "a_b_in": nrm((nA, 2 * D), 0.02),
        "a_conv_w": nrm((nA, CONV_KERNEL, D), CONV_KERNEL ** -0.5),
        "a_conv_b": nrm((nA, D), 0.02),
        "a_ln_g": gain((nA, D)),
        "a_ln_b": nrm((nA, D), 0.02),
        "a_w_out": nrm((nA, D, D), D ** -0.5),
        "a_b_out": nrm((nA, D), 0.02),
        "b_w_in": nrm((nB, D, 3 * D), D ** -0.5),
        "b_conv_w": nrm((nB, SHORT_CONV, D), SHORT_CONV ** -0.5),
        "b_w_out": nrm((nB, D, D), D ** -0.5),
        "c_w_qkv": nrm((nC, D, 3 * D), D ** -0.5),
        "c_q_norm": gain((nC, FOX_HEAD_DIM)),
        "c_k_norm": gain((nC, FOX_HEAD_DIM)),
        "c_w_f": nrm((nC, D, FOX_HEADS), 0.1 * D ** -0.5),
        "c_b_f": 2.0 + nrm((nC, FOX_HEADS), 1.0),
        "c_w_out": nrm((nC, D, D), D ** -0.5),
        "d_w_in": nrm((nD, D, 2 * GLA_DK + 2 * GLA_DV), D ** -0.5),
        "d_w_g1": nrm((nD, D, GLA_GATE_RANK), D ** -0.5),
        "d_w_g2": nrm((nD, GLA_GATE_RANK, GLA_DK), GLA_GATE_RANK ** -0.5),
        "d_b_g": nrm((nD, GLA_DK), 0.02),
        "d_o_norm": gain((nD, GLA_DV_HEAD)),
        "d_w_out": nrm((nD, GLA_DV, D), GLA_DV ** -0.5),
    }

def second_block(x, mix_norm, mlp_norm, mlp_w1, mlp_w2,
              a_w_in, a_b_in, a_conv_w, a_conv_b, a_ln_g, a_ln_b, a_w_out, a_b_out,
              b_w_in, b_conv_w, b_w_out,
              c_w_qkv, c_q_norm, c_k_norm, c_w_f, c_b_f, c_w_out,
              d_w_in, d_w_g1, d_w_g2, d_b_g, d_o_norm, d_w_out):
    for i in range(DEPTH_2):
        m, j = i % N_MIXERS_2, i // N_MIXERS_2
        h = rms_norm_2(x, mix_norm[i])
        if m == 0:
            y = conformer_conv(h, a_w_in[j], a_b_in[j], a_conv_w[j], a_conv_b[j],
                               a_ln_g[j], a_ln_b[j], a_w_out[j], a_b_out[j])
        elif m == 1:
            y = short_gated_conv(h, b_w_in[j], b_conv_w[j], b_w_out[j])
        elif m == 2:
            y = forgetting_attention(h, c_w_qkv[j], c_q_norm[j], c_k_norm[j],
                                     c_w_f[j], c_b_f[j], c_w_out[j])
        else:
            y = gated_linear_attention(h, d_w_in[j], d_w_g1[j], d_w_g2[j], d_b_g[j],
                                       d_o_norm[j], d_w_out[j])
        x = x + y
        x = x + squared_relu_mlp(rms_norm_2(x, mlp_norm[i]), mlp_w1[i], mlp_w2[i])
    return x


def setup_inputs(seed=0):
    out = dict(first_inputs(seed))
    for name, value in second_inputs(seed + 1).items():
        if name != "x":
            out[name + "_2"] = value
    return out


def reference(
    x, pool_w, pool_b, pool_scale, attn_w_qkv, attn_b_qkv, attn_sinks, attn_w_o, norm_mix,
    norm_ffn, ffn_w_in, ffn_conv_w, ffn_conv_b, ffn_w_out, norm_f, mix_norm_2, mlp_norm_2,
    mlp_w1_2, mlp_w2_2, a_w_in_2, a_b_in_2, a_conv_w_2, a_conv_b_2, a_ln_g_2, a_ln_b_2,
    a_w_out_2, a_b_out_2, b_w_in_2, b_conv_w_2, b_w_out_2, c_w_qkv_2, c_q_norm_2, c_k_norm_2,
    c_w_f_2, c_b_f_2, c_w_out_2, d_w_in_2, d_w_g1_2, d_w_g2_2, d_b_g_2, d_o_norm_2, d_w_out_2,
):
    x = first_block(
        x, pool_w, pool_b, pool_scale, attn_w_qkv, attn_b_qkv, attn_sinks, attn_w_o, norm_mix,
        norm_ffn, ffn_w_in, ffn_conv_w, ffn_conv_b, ffn_w_out, norm_f,
    )
    return second_block(
        x, mix_norm_2, mlp_norm_2, mlp_w1_2, mlp_w2_2, a_w_in_2, a_b_in_2, a_conv_w_2,
        a_conv_b_2, a_ln_g_2, a_ln_b_2, a_w_out_2, a_b_out_2, b_w_in_2, b_conv_w_2, b_w_out_2,
        c_w_qkv_2, c_q_norm_2, c_k_norm_2, c_w_f_2, c_b_f_2, c_w_out_2, d_w_in_2, d_w_g1_2,
        d_w_g2_2, d_b_g_2, d_o_norm_2, d_w_out_2,
    )


_drawn_inputs = setup_inputs


def setup_inputs(seed=0):
    import zlib

    import numpy as np

    out = dict(_drawn_inputs(seed))
    spreads = {}
    factors = {'attn_b_qkv': 3.691,
     'attn_sinks': 3.156,
     'ffn_conv_b': 3.04,
     'a_b_in_2': 4.511,
     'a_ln_b_2': 5.132,
     'a_b_out_2': 3.093}
    for name, (base, spread) in spreads.items():
        noise = np.random.default_rng([zlib.crc32(name.encode()), seed]).standard_normal(out[name].shape)
        drawn = base * np.exp(spread * noise) if base else spread * noise
        out[name] = jnp.asarray(drawn.astype(out[name].dtype))
    for name, factor in factors.items():
        out[name] = (out[name] * factor).astype(out[name].dtype)
    return out
```

```python
from contextlib import ExitStack

import numpy as np

import concourse.bass as bass
from concourse import mybir

F32 = mybir.dt.float32
F32R = mybir.dt.float32r
ALU = mybir.AluOpType
ACT = mybir.ActivationFunctionType
AX_X = mybir.AxisListType.X

P = 128
D = 1024
T = 512
C = D // P
NBLK = T // P
EPS = 1e-6
WINDOWS = (2, 4, 8, 16)
PAD = max(WINDOWS)
HEADS, KV, HD = 16, 4, 64
REP = HEADS // KV
FF_PAIRS = 2816 // P
FF_PARTS = (8, 8, 6)
MLP_PARTS = (8, 8, 8, 8)
TAPS = 31
PE_TAPS = 11
SLOTS = 4
AHEAD = 3
KT = 8
MASKED = -1.0e30

VEC_PARTS = [("pool_b", C), ("pool_scale", C), ("g_mix0", C), ("g_mix1", C), ("g_ffn0", C), ("g_ffn1", C),
             ("g_final", C), ("g_mix2", C), ("g_mlp2", C), ("b_qkv", 12), ("b_in", 2 * C), ("conv_b", C),
             ("ln_g", C), ("ln_b", C), ("b_out", C), ("sinks", HEADS), ("glu", 2 * FF_PAIRS * 8),
             ("conv_w", C * TAPS)]
VEC = {}
_at = 0
for _name, _n in VEC_PARTS:
    VEC[_name] = _at
    _at += _n
VEC_COLS = _at
CST_DIST, CST_INV, CST_ID = 0, 2 * P, 2 * P + PAD
CST_COLS = CST_ID + P


class Phase:

    def __init__(self, name, weights, units, tiles, unit, chain):
        self.name, self.weights, self.units, self.tiles = name, weights, units, tiles
        self.unit, self.chain = unit, chain
        self.end_chain = chain + (2 * units if name == "pool" else units)


def plan(w):
    phases, unit, chain = {}, 0, 0

    def add(name, weights, units, tiles):
        nonlocal unit, chain
        phases[name] = ph = Phase(name, weights, units, tiles, unit, chain)
        unit, chain = unit + units, ph.end_chain

    def add_mlp(kind, parts, per_part):
        order = [("up", 0)]
        for q in range(1, len(parts)):
            order += [("up", q), ("down", q - 1)]
        order.append(("down", len(parts) - 1))
        for what, q in order:
            if what == "up":
                add(f"{kind}_up{q}", w[f"{kind}_up{q}"], per_part * parts[q], C)
            else:
                add(f"{kind}_down{q}", w[f"{kind}_down{q}"], C, parts[q])

    add("pool", w["pool"], 4, 4)
    add_mlp("ffn0", FF_PARTS, 2)
    add("qkv", w["qkv"], 12, C)
    add("wo", w["wo"], C, C)
    add_mlp("ffn1", FF_PARTS, 2)
    add("ain", w["ain"], 2 * C, C)
    add("aout", w["aout"], C, C)
    add_mlp("mlp", MLP_PARTS, 1)
    return phases, unit, chain


def row(t, c):
    if isinstance(c, int):
        return t[:, c, :]
    return t[:, bass.ds(c, 1), :].rearrange("p o n -> p (o n)")


def col(t, e):
    return t[:, e:e + 1] if isinstance(e, int) else t[:, bass.ds(e, 1)]


def run(eng, step, n, peel_first=False, peel_last=False):
    lo, hi = int(peel_first), n - int(peel_last)
    if peel_first:
        step(0)
    if hi - lo == 1:
        step(lo)
    elif hi > lo:
        with eng.Fori(lo, hi) as i:
            step(i)
    if peel_last:
        step(n - 1)


def build(nc, xT, vec_in, cst_in, w_in, out):
    ph, UNITS, CHAINS = plan(w_in)
    order = list(ph.values())

    with ExitStack() as ctx:
        def sb(name, shape, dt=F32, scope=ctx):
            return scope.enter_context(nc.sbuf_tensor(name, shape, dt))

        def sem(name):
            return ctx.enter_context(nc.semaphore(name))

        res = sb("res", [P, C, T])
        xh = sb("xh", [P, C, T], F32R)
        xl = sb("xl", [P, C, T], F32R)
        raw = sb("raw", [P, SLOTS, KT * P])
        whi = sb("whi", [P, SLOTS, KT * P], F32R)
        wlo = sb("wlo", [P, SLOTS, KT * P], F32R)
        vec = sb("vec", [P, VEC_COLS])
        cst = sb("cst", [P, CST_COLS])
        ones = sb("ones", [P, P])
        eps = sb("eps", [P, 1])
        gfm = sb("gfm", [P, C])
        sink8 = sb("sink8", [P, HEADS])
        rms = sb("rms", [P, T])
        rinv = sb("rinv", [P, T])
        ssum = sb("ssum", [P, 2, T])
        sq = sb("sq", [P, 2, T])
        u = sb("u", [P, 4, 2 + T])
        tmp = sb("tmp", [P, 4, T])
        gate = sb("gate", [P, 2, T])
        prod = sb("prod", [P, 2, T])
        with ExitStack() as own:
            ahi = sb("ahi", [P, 2, 8, T], F32R, own)
            alo = sb("alo", [P, 2, 8, T], F32R, own)
        with ExitStack() as own:
            zp = sb("zp", [P, 3, PAD + T], F32, own)
        with ExitStack() as own:
            ohi = sb("ohi", [P, C, T], F32R, own)
        with ExitStack() as own:
            qkvT = sb("qkvT", [P, 12, T], F32, own)
            olo = sb("olo", [P, C, T], F32R, own)
            vt = sb("vt", [P, NBLK, 2, P], F32, own)
            prob = sb("prob", [P, 2, REP, 2 * P], F32, own)
            pT = sb("pT", [P, 2, 2, REP * P], F32, own)
            stat = sb("stat", [P, 6, NBLK * KV, REP], F32, own)
        with ExitStack() as own:
            ylo = sb("ylo", [P, C, T], F32R, own)
            yhi = sb("yhi", [P, C, T], F32R, own)
        with ExitStack() as own:
            hv = sb("hv", [P, C, T], F32, own)
            hc = sb("hc", [P, 2, TAPS - 1 + T], F32, own)
            hch = sb("hch", [P, 2, TAPS - 1 + T], F32R, own)
            hcl = sb("hcl", [P, 2, TAPS - 1 + T], F32R, own)
            dgh = sb("dgh", [P, 2, PE_TAPS * P], F32R, own)
            dgl = sb("dgl", [P, 2, PE_TAPS * P], F32R, own)
            cwh = sb("cwh", [P, C * TAPS], F32R, own)
            cwl = sb("cwl", [P, C * TAPS], F32, own)
            mu = sb("mu", [P, T], F32, own)
            r1 = sb("r1", [P, T], F32, own)
        bank = [ctx.enter_context(nc.psum_tensor(f"bank{b}", [P, T], F32)) for b in range(8)]
        acc = bank[0:4]
        norm = bank[4:6]

        x_in = [sem(f"x_in{q}") for q in range(4)]
        vec_loaded = sem("vec_loaded")
        cst_loaded = sem("cst_loaded")
        w_loaded = [sem(f"w_loaded{s}") for s in range(SLOTS)]
        hi_done = sem("hi_done")
        lo_done = sem("lo_done")
        chain_done = sem("chain_done")
        acc_free = sem("acc_free")
        setup = sem("setup")
        xh_ready = sem("xh_ready")
        xl_ready = sem("xl_ready")
        sq_ready = sem("sq_ready")
        ssum_ready = sem("ssum_ready")
        norm_done = sem("norm_done")
        rms_ready = sem("rms_ready")
        rinv_ready = sem("rinv_ready")
        slide = sem("slide")
        pooled = sem("pooled")
        tap2_done = sem("tap2_done")
        tap1_done = sem("tap1_done")
        tap0_done = sem("tap0_done")
        gate_ready = sem("gate_ready")
        prod_ready = sem("prod_ready")
        act_hi = sem("act_hi")
        act_lo = sem("act_lo")
        qkv_ready = sem("qkv_ready")
        vT_done = sem("vT_done")
        v_ready = sem("v_ready")
        scores_done = sem("scores_done")
        biased = sem("biased")
        max_steps = sem("max_steps")
        exp_done = sem("exp_done")
        den_steps = sem("den_steps")
        prob_ready = sem("prob_ready")
        pT_done = sem("pT_done")
        pT_ready = sem("pT_ready")
        pv_done = sem("pv_done")
        o_hi = sem("o_hi")
        o_lo = sem("o_lo")
        x2_ready = sem("x2_ready")
        sig_ready = sem("sig_ready")
        hc_ready = sem("hc_ready")
        hch_ready = sem("hch_ready")
        hcl_ready = sem("hcl_ready")
        taps_split = sem("taps_split")
        diag_ready = sem("diag_ready")
        conv_done = sem("conv_done")
        tap_steps = sem("tap_steps")
        hv_ready = sem("hv_ready")
        mean_done = sem("mean_done")
        mu_ready = sem("mu_ready")
        xc_ready = sem("xc_ready")
        xcsq_ready = sem("xcsq_ready")
        sqsum_done = sem("sqsum_done")
        ln_scaled = sem("ln_scaled")
        ln_silu = sem("ln_silu")
        ln_hi = sem("ln_hi")
        ln_lo = sem("ln_lo")
        stored = sem("stored")

        ident = cst[:, CST_ID:CST_ID + P]

        def v(name, e=0):
            return col(vec, VEC[name] + e)

        NORMS = ["pool", "ffn0", "qkv", "ffn1", "ain", "mlp"]
        GAIN = {"pool": "g_mix0", "ffn0": "g_ffn0", "qkv": "g_mix1", "ffn1": "g_ffn1", "mlp": "g_mlp2"}
        X = {name: C * k for k, name in enumerate(NORMS)}
        SS = {"pool": 0, "ffn0": 9, "qkv": 18, "ffn1": 27, "ain": 36, "mlp": 36 + 17}
        SQ = {"pool": 0, "ffn0": 8, "qkv": 16, "ffn1": 24, "ain": 32, "mlp": 48}
        ND = {"pool": 0, "ffn0": 1, "qkv": 2, "ffn1": 3, "ain": 4, "mlp": 6}
        RR = {"pool": 0, "ffn0": 1, "qkv": 2, "ffn1": 3, "ain": 4, "mlp": 7}

        pair0, act0 = {}, {}
        pairs = acts = 0
        for name in ph:
            kind, _, part = name.rpartition("_up")
            if kind.startswith("ffn"):
                pair0[name], act0[name] = pairs, acts
                pairs, acts = pairs + FF_PARTS[int(part)], acts + FF_PARTS[int(part)]
            elif kind == "mlp":
                act0[name] = acts
                acts += MLP_PARTS[int(part)]

        def used(unit):
            return 2 * unit + 2 if isinstance(unit, int) and unit < 4 else unit + 5

        def loads(base, i, k):
            return 16 * (i + (base + k) // SLOTS + 1)

        block = ctx.enter_context(nc.Block())

        @block.sync
        def _(sp):
            def load(p, i, k):
                unit = p.unit + SLOTS * i + k
                if isinstance(unit, int) and unit < SLOTS:
                    free, at = None, unit - p.unit
                elif isinstance(i, int):
                    free, at = unit - SLOTS + 1, SLOTS * i + k
                else:
                    free, at = sp.snap(unit - SLOTS + 1), sp.snap(SLOTS * i + k)
                src = p.weights[at] if isinstance(at, int) else \
                    p.weights[bass.ds(at, 1)].rearrange("o p n -> p (o n)")
                if free is not None:
                    sp.wait_ge(lo_done, free)
                sp.dma_start(raw[:, k, 0:p.tiles * P], src).then_inc(w_loaded[k], 16)

            for p in order:
                run(sp, lambda i: [load(p, i, k) for k in range(SLOTS)], p.units // SLOTS)
            last = ph["mlp_down3"]
            for c in range(C):
                sp.wait_ge(acc_free, last.chain + c + 1)
                sp.dma_start(out[:, c, :], res[:, c, :]).then_inc(stored, 16)
            sp.wait_ge(stored, 16 * C)

        @block.gpsimd
        def _(pool):
            pool.wait_ge(cst_loaded, 16)
            pool.wait_ge(taps_split, 2)
            for c in range(C):
                if c >= 2:
                    pool.wait_ge(conv_done, c - 1)
                for k in range(PE_TAPS):
                    e = c * TAPS + k
                    nc.gpsimd.tensor_scalar(dgh[:, c % 2, k * P:(k + 1) * P], ident,
                                            cwh[:, e:e + 1].bitcast(F32), None, ALU.mult)
                    last = nc.gpsimd.tensor_scalar(dgl[:, c % 2, k * P:(k + 1) * P], ident,
                                                   cwl[:, e:e + 1], None, ALU.mult)
                last.then_inc(diag_ready, 1)

        @block.tensor
        def _(pe):
            def three(out_, hi, lo, mh, ml, first, last):
                nc.tensor.matmul(out_, hi, mh, start=first, stop=False)
                nc.tensor.matmul(out_, hi, ml, start=False, stop=False)
                return nc.tensor.matmul(out_, lo, mh, start=False, stop=last)

            def chain(p, i, k, hi, lo, count_x=None):
                chain_no = p.chain + SLOTS * i + k
                pe.wait_ge(lo_done, p.unit + SLOTS * i + k + 1)
                pe.wait_ge(acc_free, chain_no - 3)
                for t in range(p.tiles):
                    if count_x is not None:
                        pe.wait_ge(xl_ready, count_x + t + 1)
                    w = slice(t * P, (t + 1) * P)
                    mm = three(acc[k][:], whi[:, k, w], wlo[:, k, w], hi[:, t, :], lo[:, t, :],
                               t == 0, t == p.tiles - 1)
                mm.then_inc(chain_done, 1)

            def sum_features(name, which=0):
                adds = 17 if name == "ain" else 9
                pe.wait_ge(ssum_ready, SS[name] + adds)
                if which == 0 and name != "pool":
                    pe.wait_ge(rms_ready, RR[name])
                nc.tensor.matmul(norm[which][:], ones[:], ssum[:, which, :], start=True, stop=True)\
                    .then_inc(norm_done, 1)

            def project(name, first):
                p = ph[name]

                def step(i):
                    peeled = first is not None and isinstance(i, int) and i == 0
                    for k in range(SLOTS):
                        chain(p, i, k, xh, xl, X[first] if peeled and k == 0 else None)
                        if peeled and k == 0:
                            sum_features(first)
                            if first == "ain":
                                sum_features(first, 1)
                run(pe, step, p.units // SLOTS, peel_first=first is not None)

            def down(name, buf, acts_before):
                p = ph[name]
                pe.wait_ge(act_lo, acts_before + p.tiles)
                run(pe, lambda i: [chain(p, i, k, ahi[:, buf], alo[:, buf]) for k in range(SLOTS)],
                    C // SLOTS)

            def feed_forward(kind, parts):
                for q in range(len(parts)):
                    project(f"{kind}_up{q}", kind if q == 0 else None)
                    if q:
                        down(f"{kind}_down{q - 1}", (q - 1) % 2, act0[f"{kind}_up{q - 1}"])
                q = len(parts) - 1
                down(f"{kind}_down{q}", q % 2, act0[f"{kind}_up{q}"])

            pe.wait_ge(setup, 1)
            for g in range(4):
                pe.wait_ge(lo_done, g + 1)
                for o in range(2):
                    c = 2 * g + o
                    if c >= 4:
                        pe.wait_ge(acc_free, c - 3)
                    for t in range(2):
                        pe.wait_ge(xl_ready, 2 * g + t + 1)
                        w = slice((2 * o + t) * P, (2 * o + t + 1) * P)
                        mm = three(acc[c % 4][:], whi[:, g, w], wlo[:, g, w], xh[:, 2 * g + t, :],
                                   xl[:, 2 * g + t, :], t == 0, t == 1)
                    mm.then_inc(chain_done, 1)
                if g == 1:
                    sum_features("pool")

            feed_forward("ffn0", FF_PARTS)

            project("qkv", "qkv")
            pe.wait_ge(qkv_ready, 12)
            pe.wait_ge(cst_loaded, 16)
            for pr in range(2):
                for n in range(NBLK):
                    mm = nc.tensor.transpose(bank[6 + pr][:, n * P:(n + 1) * P],
                                             qkvT[:, 10 + pr, n * P:(n + 1) * P], ident)
                mm.then_inc(vT_done, 1)

            STEPS = [(n, g) for n in range(NBLK) for g in range(KV)]

            def keys(n):
                return P if n == 0 else 0

            def scores(s):
                n, g = STEPS[s]
                k0, half = keys(n), slice(HD * (g % 2), HD * (g % 2) + HD)
                if s >= 2:
                    pe.wait_ge(biased, REP * (s - 1))
                for i in range(REP):
                    o = (i % 2) * 2 * P
                    mm = nc.tensor.matmul(acc[2 * (s % 2) + i // 2][:, o + k0:o + 2 * P],
                                          qkvT[half, 4 * (g // 2) + i, n * P:(n + 1) * P],
                                          qkvT[half, 8 + g // 2, (n - 1) * P + k0:(n + 1) * P],
                                          start=True, stop=True)
                mm.then_inc(scores_done, 1)

            def transposes(s):
                n, _ = STEPS[s]
                pe.wait_ge(prob_ready, REP * (s + 1))
                if s >= 1:
                    pe.wait_ge(pT_ready, s)
                for b in range(keys(n) // P, 2):
                    for i in range(REP):
                        mm = nc.tensor.transpose(bank[4 + b][:, i * P:(i + 1) * P],
                                                 prob[:, s % 2, i, b * P:(b + 1) * P], ident)
                mm.then_inc(pT_done, 1)

            def values(s):
                n, g = STEPS[s]
                pe.wait_ge(pT_ready, s + 1)
                if s == 0:
                    pe.wait_ge(v_ready, 2)
                if s >= 4 and g % 2 == 0:
                    pe.wait_ge(o_lo, s // 2 - 1)
                half = slice(HD * (g % 2), HD * (g % 2) + HD)
                for b in range(keys(n) // P, 2):
                    mm = nc.tensor.matmul(bank[6 + (s // 2) % 2][half, :], vt[:, n - 1 + b, g // 2, half],
                                          pT[:, s % 2, b, :], start=(b == keys(n) // P), stop=(b == 1))
                mm.then_inc(pv_done, 1)

            scores(0)
            for s in range(len(STEPS)):
                if s + 1 < len(STEPS):
                    scores(s + 1)
                if s >= 1:
                    values(s - 1)
                transposes(s)
            values(len(STEPS) - 1)

            pe.wait_ge(o_lo, NBLK * 2)
            pe.wait_ge(biased, REP * len(STEPS))
            p = ph["wo"]
            run(pe, lambda i: [chain(p, i, k, ohi, olo) for k in range(SLOTS)], p.units // SLOTS)

            feed_forward("ffn1", FF_PARTS)

            p = ph["ain"]

            def convolve(c):
                b = c % 2
                pe.wait_ge(hcl_ready, c + 1)
                pe.wait_ge(diag_ready, c + 1)
                if c >= 2:
                    pe.wait_ge(hv_ready, c - 1)
                for k in range(PE_TAPS):
                    w = slice(k * P, (k + 1) * P)
                    mm = three(bank[6 + b][:], dgh[:, b, w], dgl[:, b, w], hch[:, b, k:k + T],
                               hcl[:, b, k:k + T], k == 0, k == PE_TAPS - 1)
                mm.then_inc(conv_done, 1)

            def feature_sum(c):
                if c == 0:
                    pe.wait_ge(rms_ready, RR["ain"] + 2)
                pe.wait_ge(hv_ready, c + 1)
                mm = nc.tensor.matmul(norm[0][:], ones[:], hv[:, c, :], start=(c == 0), stop=(c == C - 1))
                if c == C - 1:
                    mm.then_inc(mean_done, 1)

            for c in range(C):
                for k in (2 * (c % 2), 2 * (c % 2) + 1):
                    chain(p, c // 2, k, xh, xl, X["ain"] if c == 0 and k == 0 else None)
                    if c == 0 and k == 0:
                        sum_features("ain")
                        sum_features("ain", 1)
                if c >= 2:
                    feature_sum(c - 2)
                if c >= 1:
                    convolve(c - 1)
            feature_sum(C - 2)
            convolve(C - 1)
            feature_sum(C - 1)
            for c in range(C):
                pe.wait_ge(xcsq_ready, c + 1)
                mm = nc.tensor.matmul(norm[1][:], ones[:], sq[:, c % 2, :], start=(c == 0), stop=(c == C - 1))
                mm.then_inc(sqsum_done, 1)
            p = ph["aout"]
            for k in range(p.units):
                pe.wait_ge(lo_done, p.unit + k + 1)
                pe.wait_ge(acc_free, p.chain + k - 3)
                for t in range(C):
                    if k == 0:
                        pe.wait_ge(ln_lo, t + 1)
                    w = slice(t * P, (t + 1) * P)
                    mm = three(acc[k % 4][:], whi[:, k % 4, w], wlo[:, k % 4, w], yhi[:, t, :], ylo[:, t, :],
                               t == 0, t == C - 1)
                mm.then_inc(chain_done, 1)

            feed_forward("mlp", MLP_PARTS)

        @block.scalar
        def _(act):
            def split_hi(base, i, k, tiles=KT):
                if isinstance(i, int) and base + SLOTS * i + k >= UNITS:
                    return
                s, unit = k % SLOTS, base + SLOTS * i + k
                act.wait_ge(w_loaded[s], loads(base, i, k))
                if not (isinstance(unit, int) and unit < SLOTS):
                    act.wait_ge(chain_done, used(unit - SLOTS))
                nc.scalar.activation(whi[:, s, 0:tiles * P], raw[:, s, 0:tiles * P], ACT.Copy)\
                    .then_inc(hi_done, 1)

            def prepare(name, c, buf, reads_done):
                if name == "ain":
                    gain = col(gfm, c)
                else:
                    gain = v(GAIN[name], c)
                if reads_done:
                    act.wait_ge(chain_done, reads_done)
                nc.scalar.activation(row(xh, c), row(res, c), ACT.Copy, scale=gain).then_inc(xh_ready, 1)
                if name == "ain":
                    nc.scalar.activation(sq[:, 0, :], row(res, c), ACT.Square).then_inc(sq_ready, 1)
                    nc.scalar.activation(sq[:, 1, :], row(res, c), ACT.Square, scale=v("g_final", c))\
                        .then_inc(sq_ready, 1)
                else:
                    nc.scalar.activation(sq[:, buf, :], row(res, c), ACT.Square).then_inc(sq_ready, 1)

            def root(count, which=0):
                act.wait_ge(norm_done, count)
                nc.scalar.activation(rms[:], norm[which][:], ACT.Sqrt, scale=1.0 / D, bias=eps[:])\
                    .then_inc(rms_ready, 1)

            def finish(name, norm_name, reads_done):
                p = ph[name]

                def step(i):
                    for k in range(SLOTS):
                        split_hi(p.unit, i, k + AHEAD)
                        act.wait_ge(acc_free, p.chain + SLOTS * i + k + 1)
                        prepare(norm_name, SLOTS * i + k, k % 2, reads_done)
                run(act, step, C // SLOTS)

            def plain(name, peel_last=False):
                p = ph[name]
                run(act, lambda i: [split_hi(p.unit, i, k + AHEAD) for k in range(SLOTS)], p.units // SLOTS,
                    peel_last=peel_last)

            def ffn_up(name, layer, buf, first, buffer_free):
                p = ph[name]
                pair_base, act_base, q0 = pair0[name], act0[name], pair0[name] % FF_PAIRS

                def step(i):
                    for b in range(2):
                        pair = pair_base + 2 * i + b
                        for j in range(2):
                            k = 2 * b + j
                            split_hi(p.unit, i, k + AHEAD)
                            if first and isinstance(i, int) and i == 0 and k == 0:
                                root(ND[first] + 1)
                            par = VEC["glu"] + ((layer * FF_PAIRS + q0) * 2 + k) * 4 + 16 * i
                            act.wait_ge(acc_free, p.chain + SLOTS * i + k + 1)
                            act.wait_ge(vec_loaded, 16)
                            nc.scalar.activation(tmp[:, k, :], u[:, k, 2:2 + T], ACT.Identity,
                                                 scale=col(vec, par + 2), bias=col(vec, par + 3))\
                                .then_inc(tap2_done, 1)
                        act.wait_ge(tap0_done, 2 * pair + 2)
                        nc.scalar.activation(gate[:, b, :], tmp[:, 2 * b + 1, :], ACT.Silu)\
                            .then_inc(gate_ready, 1)
                        act.wait_ge(prod_ready, act_base + 2 * i + b + 1)
                        act.wait_ge(chain_done, buffer_free)
                        nc.scalar.activation(row(ahi[:, buf], 2 * i + b), prod[:, b, :], ACT.Copy)\
                            .then_inc(act_hi, 1)
                run(act, step, p.units // SLOTS, peel_first=bool(first))

            def mlp_up(name, buf, first, buffer_free):
                p, act_base = ph[name], act0[name]

                def step(i):
                    for k in range(SLOTS):
                        split_hi(p.unit, i, k + AHEAD)
                        if first and isinstance(i, int) and i == 0 and k == 0:
                            root(ND[first] + 1)
                        act.wait_ge(prod_ready, act_base + SLOTS * i + k + 1)
                        act.wait_ge(chain_done, buffer_free)
                        nc.scalar.activation(row(ahi[:, buf], SLOTS * i + k), tmp[:, k, :], ACT.Copy)\
                            .then_inc(act_hi, 1)
                run(act, step, p.units // SLOTS, peel_first=bool(first))

            def feed_forward(kind, parts, layer, next_norm):
                n = len(parts)
                for q in range(n):
                    up = f"{kind}_up{q}"
                    free = ph[f"{kind}_down{q - 2}"].end_chain if q >= 2 else ph[up].chain
                    if kind == "mlp":
                        mlp_up(up, q % 2, kind if q == 0 else None, free)
                    else:
                        ffn_up(up, layer, q % 2, kind if q == 0 else None, free)
                    if q:
                        plain(f"{kind}_down{q - 1}")
                if next_norm:
                    finish(f"{kind}_down{n - 1}", next_norm, ph[f"{kind}_up{n - 1}"].end_chain)
                else:
                    plain(f"{kind}_down{n - 1}", peel_last=True)

            act.dma_start(vec[:], vec_in).then_inc(vec_loaded, 16)
            for q in range(4):
                act.dma_start(res[:, 2 * q:2 * q + 2, :], xT[:, 2 * q:2 * q + 2, :]).then_inc(x_in[q], 16)
            act.dma_start(cst[:], cst_in).then_inc(cst_loaded, 16)

            act.wait_ge(setup, 1)
            act.wait_ge(vec_loaded, 16)
            for c in range(C):
                if c % 2 == 0:
                    act.wait_ge(x_in[c // 2], 16)
                if c >= 2:
                    act.wait_ge(ssum_ready, c)
                prepare("pool", c, c % 2, 0)
                if c in (1, 3, 5):
                    split_hi(0, 0, c // 2, 4)
            root(1)
            for c in range(C):
                if c % 2 == 0:
                    split_hi(0, 0, c // 2 + AHEAD, 4 if c == 0 else KT)
                act.wait_ge(pooled, c + 1)
                prepare("ffn0", c, c % 2, 2 * (c // 2) + 2)

            feed_forward("ffn0", FF_PARTS, 0, "qkv")

            p = ph["qkv"]

            def qkv_step(i):
                for k in range(SLOTS):
                    split_hi(p.unit, i, k + AHEAD)
                    if isinstance(i, int) and k == 0:
                        root(ND["qkv"] + 1)
                    m = SLOTS * i + k
                    act.wait_ge(acc_free, p.chain + m + 1)
                    act.wait_ge(vec_loaded, 16)
                    nc.scalar.activation(row(qkvT, m), tmp[:, k, :], ACT.Identity, bias=v("b_qkv", m))\
                        .then_inc(qkv_ready, 1)
            run(act, qkv_step, 3, peel_first=True)
            for pr in range(2):
                act.wait_ge(vT_done, pr + 1)
                nc.scalar.activation(vt[:, :, pr, :], bank[6 + pr][:].rearrange("p (n d) -> p n d", n=NBLK),
                                     ACT.Copy).then_inc(v_ready, 1)

            def exps(s):
                n, g = s // KV, s % KV
                k0 = P if n == 0 else 0
                act.wait_ge(max_steps, 4 * (s + 1))
                for i in range(REP):
                    a = prob[:, s % 2, i, k0:2 * P]
                    nc.scalar.activation(a, a, ACT.Exp, scale=HD ** -0.5, bias=stat[:, 1, s, i:i + 1],
                                         accum_out=stat[:, 3, s, i:i + 1])
                nc.scalar.activation(stat[:, 4, s, :], stat[:, 2, s, :], ACT.Exp, scale=HD ** -0.5)\
                    .then_inc(exp_done, 1)

            def copy_pT(s):
                b0 = 1 if s // KV == 0 else 0
                act.wait_ge(pT_done, s + 1)
                if s >= 2:
                    act.wait_ge(pv_done, s - 1)
                for b in range(b0, 2):
                    last = nc.scalar.activation(pT[:, s % 2, b, :], bank[4 + b][:], ACT.Copy)
                last.then_inc(pT_ready, 1)

            def out_hi(s):
                n, pr = s // KV, (s % KV) // 2
                act.wait_ge(pv_done, s + 1)
                nc.scalar.activation(ohi[:, 4 * pr:4 * pr + 4, n * P:(n + 1) * P],
                                     bank[6 + (s // 2) % 2][:].rearrange("p (i q) -> p i q", i=REP), ACT.Copy)\
                    .then_inc(o_hi, 1)

            N = NBLK * KV
            exps(0)
            for s in range(N):
                if s + 1 < N:
                    exps(s + 1)
                if s >= 2 and s % 2 == 0:
                    out_hi(s - 1)
                copy_pT(s)
            out_hi(N - 1)
            finish("wo", "ffn1", ph["qkv"].end_chain)

            feed_forward("ffn1", FF_PARTS, 1, "ain")

            nc.scalar.activation(cwh[:], vec[:, VEC["conv_w"]:VEC["conv_w"] + C * TAPS], ACT.Copy)\
                .then_inc(taps_split, 1)
            p = ph["ain"]
            for c in range(C):
                for j in range(2):
                    split_hi(p.unit, 0, 2 * c + j + AHEAD)
                    if c == 0 and j == 0:
                        root(ND["ain"] + 1)
                        act.wait_ge(rinv_ready, 7)
                        nc.scalar.activation(rms[:], rms[:], ACT.Sqrt, scale=1.0 / D, bias=eps[:])\
                            .then_inc(rms_ready, 1)
                act.wait_ge(acc_free, p.chain + 2 * c + 2)
                nc.scalar.activation(gate[:, c % 2, :], tmp[:, 2 * (c % 2) + 1, :], ACT.Sigmoid,
                                     bias=v("b_in", C + c)).then_inc(sig_ready, 1)
                act.wait_ge(hc_ready, c + 1)
                if c >= 2:
                    act.wait_ge(conv_done, c - 1)
                nc.scalar.activation(hch[:, c % 2, :], hc[:, c % 2, :], ACT.Copy).then_inc(hch_ready, 1)
            act.wait_ge(mean_done, 1)
            nc.scalar.activation(mu[:], norm[0][:], ACT.Copy, scale=1.0 / D).then_inc(mu_ready, 1)
            for c in range(C):
                act.wait_ge(xc_ready, c + 1)
                if c >= 2:
                    act.wait_ge(sqsum_done, c - 1)
                nc.scalar.activation(sq[:, c % 2, :], hv[:, c, :], ACT.Square).then_inc(xcsq_ready, 1)
            act.wait_ge(sqsum_done, C)
            nc.scalar.activation(rms[:], norm[1][:], ACT.Sqrt, scale=1.0 / D, bias=eps[:]).then_inc(rms_ready, 1)
            for c in range(C):
                act.wait_ge(ln_scaled, c + 1)
                nc.scalar.activation(hv[:, c, :], hv[:, c, :], ACT.Silu, scale=v("ln_g", c), bias=v("ln_b", c))\
                    .then_inc(ln_silu, 1)
                act.wait_ge(ln_silu, c + 1)
                nc.scalar.activation(yhi[:, c, :], hv[:, c, :], ACT.Copy).then_inc(ln_hi, 1)
            finish("aout", "mlp", ph["ain"].end_chain)

            feed_forward("mlp", MLP_PARTS, None, None)

        @block.vector
        def _(dve):
            V = nc.vector

            def split_lo(base, i, k, tiles=KT):
                if isinstance(i, int) and base + SLOTS * i + k >= UNITS:
                    return
                s = k % SLOTS
                dve.wait_ge(hi_done, base + SLOTS * i + k + 1)
                V.tensor_tensor(wlo[:, s, 0:tiles * P], raw[:, s, 0:tiles * P],
                                whi[:, s, 0:tiles * P].bitcast(F32), ALU.subtract).then_inc(lo_done, 1)

            def prepare(name, c, buf, reads=True):
                gain = col(gfm, c) if name == "ain" else v(GAIN[name], c)
                dve.wait_ge(xh_ready, X[name] + c + 1)
                V.scalar_tensor_tensor(row(xl, c), row(res, c), gain, row(xh, c).bitcast(F32),
                                       op0=ALU.mult, op1=ALU.subtract).then_inc(xl_ready, 1)
                for which in range(2 if name == "ain" else 1):
                    per = 2 if name == "ain" else 1
                    src = which if name == "ain" else buf
                    dve.wait_ge(sq_ready, SQ[name] + per * c + which + 1)
                    dve.wait_ge(ssum_ready, SS[name] + per * c + which + 1)
                    V.tensor_tensor(ssum[:, which, :], ssum[:, which, :], sq[:, src, :], ALU.add)\
                        .then_inc(ssum_ready, 1)

            def invert(name, k0):
                dve.wait_ge(rms_ready, RR[name] + 1)
                V.reciprocal(rinv[:], rms[:]).then_inc(rinv_ready, 1)
                V.memset(ssum[:], 0.0).then_inc(ssum_ready, 1)
                dve.wait_ge(rinv_ready, k0)

            def add_residual(p, i, k):
                c = SLOTS * i + k
                dve.wait_ge(chain_done, p.chain + c + 1)
                V.tensor_tensor(row(res, c), acc[k][:], row(res, c), ALU.add).then_inc(acc_free, 1)

            def finish(name, norm_name, bias=None):
                p = ph[name]

                def step(i):
                    for k in range(SLOTS):
                        c = SLOTS * i + k
                        split_lo(p.unit, i, k + AHEAD)
                        if bias:
                            dve.wait_ge(chain_done, p.chain + c + 1)
                            V.scalar_tensor_tensor(row(res, c), acc[k][:], v(bias, c), row(res, c),
                                                   op0=ALU.add, op1=ALU.add).then_inc(acc_free, 1)
                        else:
                            add_residual(p, i, k)
                        prepare(norm_name, c, k % 2)
                run(dve, step, C // SLOTS)

            def plain_down(name, peel_last=False):
                p = ph[name]

                def step(i):
                    for k in range(SLOTS):
                        split_lo(p.unit, i, k + AHEAD)
                        add_residual(p, i, k)
                run(dve, step, C // SLOTS, peel_last=peel_last)

            def ffn_up(name, layer, buf, first, rinv_count):
                p = ph[name]
                pair_base, act_base, q0 = pair0[name], act0[name], pair0[name] % FF_PAIRS

                def step(i):
                    for b in range(2):
                        pair = pair_base + 2 * i + b
                        par = VEC["glu"] + ((layer * FF_PAIRS + q0) * 2 + 2 * b) * 4 + 16 * i
                        split_lo(p.unit, i, 2 * b + AHEAD)
                        if first and isinstance(i, int) and i == 0 and b == 0:
                            invert(first, rinv_count)
                        for j in range(2):
                            k = 2 * b + j
                            dve.wait_ge(chain_done, p.chain + SLOTS * i + k + 1)
                            V.tensor_tensor(u[:, k, 2:2 + T], acc[k][:], rinv[:], ALU.mult).then_inc(acc_free, 1)
                        for shift, done, before in ((1, tap1_done, tap2_done), (0, tap0_done, tap1_done)):
                            for j in range(2):
                                k = 2 * b + j
                                dve.wait_ge(before, 2 * pair + j + 1)
                                V.scalar_tensor_tensor(tmp[:, k, :], u[:, k, shift:shift + T],
                                                       col(vec, par + 4 * j + shift), tmp[:, k, :],
                                                       op0=ALU.mult, op1=ALU.add).then_inc(done, 1)
                        split_lo(p.unit, i, 2 * b + 1 + AHEAD)
                        dve.wait_ge(gate_ready, pair + 1)
                        V.tensor_tensor(prod[:, b, :], tmp[:, 2 * b, :], gate[:, b, :], ALU.mult)\
                            .then_inc(prod_ready, 1)
                        dve.wait_ge(act_hi, act_base + 2 * i + b + 1)
                        V.tensor_tensor(row(alo[:, buf], 2 * i + b), prod[:, b, :],
                                        row(ahi[:, buf], 2 * i + b).bitcast(F32), ALU.subtract)\
                            .then_inc(act_lo, 1)
                run(dve, step, p.units // SLOTS, peel_first=bool(first))

            def mlp_up(name, buf, first, rinv_count):
                p, act_base = ph[name], act0[name]

                def step(i):
                    for k in range(SLOTS):
                        split_lo(p.unit, i, k + AHEAD)
                        if first and isinstance(i, int) and i == 0 and k == 0:
                            invert(first, rinv_count)
                        a = act_base + SLOTS * i + k
                        dve.wait_ge(chain_done, p.chain + SLOTS * i + k + 1)
                        V.tensor_tensor(u[:, k, 2:2 + T], acc[k][:], rinv[:], ALU.mult).then_inc(acc_free, 1)
                        dve.wait_ge(acc_free, p.chain + SLOTS * i + k + 1)
                        V.scalar_tensor_tensor(tmp[:, k, :], u[:, k, 2:2 + T], 0.0, u[:, k, 2:2 + T],
                                               op0=ALU.max, op1=ALU.mult).then_inc(prod_ready, 1)
                        dve.wait_ge(act_hi, a + 1)
                        V.tensor_tensor(row(alo[:, buf], SLOTS * i + k), tmp[:, k, :],
                                        row(ahi[:, buf], SLOTS * i + k).bitcast(F32), ALU.subtract)\
                            .then_inc(act_lo, 1)
                run(dve, step, p.units // SLOTS, peel_first=bool(first))

            def feed_forward(kind, parts, layer, next_norm, rinv_count):
                n = len(parts)
                for q in range(n):
                    if kind == "mlp":
                        mlp_up(f"{kind}_up{q}", q % 2, kind if q == 0 else None, rinv_count)
                    else:
                        ffn_up(f"{kind}_up{q}", layer, q % 2, kind if q == 0 else None, rinv_count)
                    if q:
                        plain_down(f"{kind}_down{q - 1}")
                if next_norm:
                    finish(f"{kind}_down{n - 1}", next_norm)
                else:
                    plain_down(f"{kind}_down{n - 1}", peel_last=True)

            V.memset(ones[:], 1.0)
            V.memset(eps[:], EPS)
            V.memset(u[:], 0.0)
            V.memset(zp[:], 0.0)
            V.memset(ssum[:], 0.0).then_inc(ssum_ready, 1)
            dve.wait_ge(ssum_ready, 1)
            dve.wait_ge(vec_loaded, 16)
            V.tensor_tensor(gfm[:], vec[:, VEC["g_final"]:VEC["g_final"] + C],
                            vec[:, VEC["g_mix2"]:VEC["g_mix2"] + C], ALU.mult)
            V.tensor_scalar(sink8[:], vec[:, VEC["sinks"]:VEC["sinks"] + HEADS], HD ** 0.5, None, ALU.mult)\
                .then_inc(setup, 1)

            for c in range(C):
                prepare("pool", c, c % 2)
                if c in (1, 3, 5):
                    split_lo(0, 0, c // 2, 4)
            invert("pool", 1)
            dve.wait_ge(cst_loaded, 16)
            steps = 0

            def stepped(ins):
                nonlocal steps
                steps += 1
                ins.then_inc(slide, 1)
                dve.wait_ge(slide, steps)

            z, tok = zp[:, 0, :], slice(PAD, PAD + T)
            for c in range(C):
                win = WINDOWS[c // 2]
                if c % 2 == 0:
                    split_lo(0, 0, c // 2 + AHEAD, 4 if c == 0 else KT)
                dve.wait_ge(chain_done, c + 1)
                V.tensor_tensor(z[:, tok], acc[c % 4][:], rinv[:], ALU.mult).then_inc(acc_free, 1)
                dve.wait_ge(acc_free, c + 1)
                src, shift, dst = z, 1, 1
                while shift < win:
                    stepped(V.tensor_tensor(zp[:, dst, tok], src[:, tok], src[:, PAD - shift:PAD - shift + T],
                                            ALU.add))
                    src, shift, dst = zp[:, dst, :], 2 * shift, 3 - dst
                V.scalar_tensor_tensor(tmp[:, 0, :], src[:, tok], 1.0 / win, z[:, tok],
                                       op0=ALU.mult, op1=ALU.subtract)
                e = win - 1
                stepped(V.tensor_tensor(tmp[:, 1, 0:e], src[:, PAD:PAD + e], cst[:, CST_INV:CST_INV + e], ALU.mult))
                stepped(V.tensor_tensor(tmp[:, 0, 0:e], tmp[:, 1, 0:e], z[:, PAD:PAD + e], ALU.subtract))
                stepped(V.tensor_scalar(tmp[:, 0, :], tmp[:, 0, :], v("pool_b", c), v("pool_scale", c),
                                        ALU.add, ALU.mult))
                V.tensor_tensor(res[:, c, :], res[:, c, :], tmp[:, 0, :], ALU.add).then_inc(pooled, 1)
                dve.wait_ge(pooled, c + 1)
                prepare("ffn0", c, c % 2)

            feed_forward("ffn0", FF_PARTS, 0, "qkv", 2)

            p = ph["qkv"]

            def qkv_step(i):
                for k in range(SLOTS):
                    split_lo(p.unit, i, k + AHEAD)
                    if isinstance(i, int) and k == 0:
                        invert("qkv", 3)
                    dve.wait_ge(chain_done, p.chain + SLOTS * i + k + 1)
                    if not isinstance(i, int):
                        dve.wait_ge(qkv_ready, SLOTS * i + k - 3)
                    V.tensor_tensor(tmp[:, k, :], acc[k][:], rinv[:], ALU.mult).then_inc(acc_free, 1)
            run(dve, qkv_step, 3, peel_first=True)

            def front(s):
                n, g = s // KV, s % KV
                k0 = P if n == 0 else 0
                dve.wait_ge(scores_done, s + 1)
                if s >= 2:
                    dve.wait_ge(pT_done, s - 1)
                for i in range(REP):
                    slope8 = float(np.float32(2.0 ** (-8.0 / HEADS * (REP * g + i + 1)))) * HD ** 0.5
                    o = (i % 2) * 2 * P
                    V.scalar_tensor_tensor(prob[:, s % 2, i, k0:2 * P], cst[:, CST_DIST + k0:CST_DIST + 2 * P],
                                           slope8, acc[2 * (s % 2) + i // 2][:, o + k0:o + 2 * P],
                                           op0=ALU.mult, op1=ALU.add).then_inc(biased, 1)
                dve.wait_ge(biased, REP * (s + 1))
                V.tensor_reduce(stat[:, 0, s, :], prob[:, s % 2, :, k0:2 * P], AX_X, ALU.max).then_inc(max_steps, 1)
                dve.wait_ge(max_steps, 4 * s + 1)
                V.tensor_tensor(stat[:, 0, s, :], stat[:, 0, s, :], sink8[:, REP * g:REP * (g + 1)], ALU.max)\
                    .then_inc(max_steps, 1)
                dve.wait_ge(max_steps, 4 * s + 2)
                V.tensor_scalar(stat[:, 1, s, :], stat[:, 0, s, :], -(HD ** -0.5), None, ALU.mult)\
                    .then_inc(max_steps, 1)
                V.tensor_tensor(stat[:, 2, s, :], sink8[:, REP * g:REP * (g + 1)], stat[:, 0, s, :], ALU.subtract)\
                    .then_inc(max_steps, 1)

            def back(s):
                k0 = P if s // KV == 0 else 0
                dve.wait_ge(exp_done, s + 1)
                V.tensor_tensor(stat[:, 4, s, :], stat[:, 3, s, :], stat[:, 4, s, :], ALU.add).then_inc(den_steps, 1)
                dve.wait_ge(den_steps, 2 * s + 1)
                V.reciprocal(stat[:, 5, s, :], stat[:, 4, s, :]).then_inc(den_steps, 1)
                dve.wait_ge(den_steps, 2 * s + 2)
                for i in range(REP):
                    a = prob[:, s % 2, i, k0:2 * P]
                    V.tensor_scalar(a, a, stat[:, 5, s, i:i + 1], None, ALU.mult).then_inc(prob_ready, 1)

            def out_lo(s):
                n, pr = s // KV, (s % KV) // 2
                at = (slice(None), slice(4 * pr, 4 * pr + 4), slice(n * P, (n + 1) * P))
                dve.wait_ge(o_hi, s // 2 + 1)
                V.tensor_tensor(olo[at], bank[6 + (s // 2) % 2][:].rearrange("p (i q) -> p i q", i=REP),
                                ohi[at].bitcast(F32), ALU.subtract).then_inc(o_lo, 1)

            N = NBLK * KV
            front(0)
            for s in range(N):
                if s + 1 < N:
                    front(s + 1)
                if s >= 2 and s % 2 == 0:
                    out_lo(s - 1)
                back(s)
            out_lo(N - 1)
            finish("wo", "ffn1")

            feed_forward("ffn1", FF_PARTS, 1, "ain", 4)

            p = ph["ain"]
            dve.wait_ge(taps_split, 1)
            V.tensor_tensor(cwl[:], vec[:, VEC["conv_w"]:VEC["conv_w"] + C * TAPS], cwh[:].bitcast(F32),
                            ALU.subtract).then_inc(taps_split, 1)
            V.memset(hc[:], 0.0).then_inc(x2_ready, 1)
            for c in range(C):
                b = c % 2
                for j in range(2):
                    split_lo(p.unit, 0, 2 * c + j + AHEAD)
                    if c == 0 and j == 0:
                        dve.wait_ge(rms_ready, RR["ain"] + 1)
                        V.reciprocal(r1[:], rms[:]).then_inc(rinv_ready, 1)
                        dve.wait_ge(norm_done, ND["ain"] + 2)
                        dve.wait_ge(rinv_ready, 5)
                        V.tensor_tensor(mu[:], norm[1][:], r1[:], ALU.mult).then_inc(rinv_ready, 1)
                        dve.wait_ge(rinv_ready, 6)
                        V.tensor_tensor(rms[:], mu[:], r1[:], ALU.mult).then_inc(rinv_ready, 1)
                        V.memset(ssum[:], 0.0).then_inc(ssum_ready, 1)
                        for d in range(C):
                            V.scalar_tensor_tensor(res[:, d, :], res[:, d, :], v("g_final", d), r1[:],
                                                   op0=ALU.mult, op1=ALU.mult).then_inc(x2_ready, 1)
                        dve.wait_ge(rms_ready, RR["ain"] + 2)
                        V.reciprocal(rinv[:], rms[:]).then_inc(rinv_ready, 1)
                        dve.wait_ge(rinv_ready, 8)
                        V.tensor_tensor(rinv[:], rinv[:], r1[:], ALU.mult).then_inc(rinv_ready, 1)
                        dve.wait_ge(rinv_ready, 9)
                    k = 2 * b + j
                    dve.wait_ge(chain_done, p.chain + 2 * c + j + 1)
                    V.tensor_tensor(tmp[:, k, :], acc[k][:], rinv[:], ALU.mult).then_inc(acc_free, 1)
                dve.wait_ge(sig_ready, c + 1)
                dve.wait_ge(x2_ready, 1)
                V.scalar_tensor_tensor(hc[:, b, TAPS - 1:TAPS - 1 + T], tmp[:, 2 * b, :], v("b_in", c),
                                       gate[:, b, :], op0=ALU.add, op1=ALU.mult).then_inc(hc_ready, 1)
                dve.wait_ge(hc_ready, c + 1)
                at = c * (TAPS - PE_TAPS)
                V.tensor_scalar(hv[:, c, :], hc[:, b, PE_TAPS:PE_TAPS + T],
                                v("conv_w", c * TAPS + PE_TAPS), v("conv_b", c), ALU.mult, ALU.add)\
                    .then_inc(tap_steps, 1)
                dve.wait_ge(hch_ready, c + 1)
                V.tensor_tensor(hcl[:, b, :], hc[:, b, :], hch[:, b, :].bitcast(F32), ALU.subtract)\
                    .then_inc(hcl_ready, 1)
                for n, k in enumerate(range(PE_TAPS + 1, TAPS)):
                    dve.wait_ge(tap_steps, at + n + 1)
                    V.scalar_tensor_tensor(hv[:, c, :], hc[:, b, k:k + T], v("conv_w", c * TAPS + k),
                                           hv[:, c, :], op0=ALU.mult, op1=ALU.add).then_inc(tap_steps, 1)
                dve.wait_ge(tap_steps, at + TAPS - PE_TAPS)
                dve.wait_ge(conv_done, c + 1)
                V.tensor_tensor(hv[:, c, :], bank[6 + b][:], hv[:, c, :], ALU.add).then_inc(hv_ready, 1)
            dve.wait_ge(mu_ready, 1)
            for c in range(C):
                V.tensor_tensor(hv[:, c, :], hv[:, c, :], mu[:], ALU.subtract).then_inc(xc_ready, 1)
            dve.wait_ge(rms_ready, RR["mlp"])
            V.reciprocal(rinv[:], rms[:]).then_inc(rinv_ready, 1)
            dve.wait_ge(rinv_ready, 10)
            for c in range(C):
                V.tensor_tensor(hv[:, c, :], hv[:, c, :], rinv[:], ALU.mult).then_inc(ln_scaled, 1)
                if c >= 2:
                    dve.wait_ge(ln_hi, c - 1)
                    V.tensor_tensor(ylo[:, c - 2, :], hv[:, c - 2, :], yhi[:, c - 2, :].bitcast(F32),
                                    ALU.subtract).then_inc(ln_lo, 1)
            for c in (C - 2, C - 1):
                dve.wait_ge(ln_hi, c + 1)
                V.tensor_tensor(ylo[:, c, :], hv[:, c, :], yhi[:, c, :].bitcast(F32), ALU.subtract)\
                    .then_inc(ln_lo, 1)
            finish("aout", "mlp", bias="b_out")

            feed_forward("mlp", MLP_PARTS, None, None, 11)


def _units(w):
    k, n = w.shape
    return np.ascontiguousarray(w.reshape(k // P, P, n // P, P).transpose(2, 1, 0, 3).reshape(n // P, P, k))


def _cols(v_):
    return v_.reshape(-1, P).T


def kernel(**inputs):
    import concourse.bacc as _bacc
    from concourse.bass_utils import run_bass_kernel_spmd as _run

    a = {k: np.asarray(t) for k, t in inputs.items()}
    w = {}
    w["pool"] = np.ascontiguousarray(
        a["pool_w"][0].reshape(4, 2, P, 2, P).transpose(0, 2, 3, 1, 4).reshape(4, P, 4 * P))
    for layer in range(2):
        wi = a["ffn_w_in"][layer].reshape(D, 2, FF_PAIRS, P).transpose(0, 2, 1, 3).reshape(D, -1)
        at = 0
        for q, n in enumerate(FF_PARTS):
            w[f"ffn{layer}_up{q}"] = _units(wi[:, 2 * at * P:2 * (at + n) * P])
            w[f"ffn{layer}_down{q}"] = _units(a["ffn_w_out"][layer][at * P:(at + n) * P])
            at += n
    heads = [8 * pr + REP * half + i for pr in range(2) for i in range(REP) for half in range(2)]
    nq = HEADS * HD

    def by_head(t):
        return t.reshape(t.shape[:-1] + (HEADS, HD))[..., heads, :].reshape(t.shape)

    wqkv, bqkv = a["attn_w_qkv"][0], a["attn_b_qkv"][0]
    w["qkv"] = _units(np.concatenate([by_head(wqkv[:, :nq]), wqkv[:, nq:]], axis=1))
    bq = np.concatenate([by_head(bqkv[:nq]), bqkv[nq:]])
    w["wo"] = _units(a["attn_w_o"][0].reshape(HEADS, HD, D)[heads].reshape(D, D))
    w["ain"] = _units(a["a_w_in_2"][0].reshape(D, 2, C, P).transpose(0, 2, 1, 3).reshape(D, -1))
    w["aout"] = _units(a["a_w_out_2"][0])
    at = 0
    for q, n in enumerate(MLP_PARTS):
        w[f"mlp_up{q}"] = _units(a["mlp_w1_2"][0][:, at * P:(at + n) * P])
        w[f"mlp_down{q}"] = _units(a["mlp_w2_2"][0][at * P:(at + n) * P])
        at += n

    glu = np.stack([*a["ffn_conv_w"].transpose(1, 0, 2), a["ffn_conv_b"]], axis=1)
    glu = glu.reshape(2, 4, 2, FF_PAIRS, P).transpose(4, 0, 3, 2, 1).reshape(P, -1)
    parts = {
        "pool_b": _cols(a["pool_b"][0].reshape(-1)), "pool_scale": _cols(a["pool_scale"][0]),
        "g_mix0": _cols(a["norm_mix"][0]), "g_mix1": _cols(a["norm_mix"][1]),
        "g_ffn0": _cols(a["norm_ffn"][0]), "g_ffn1": _cols(a["norm_ffn"][1]),
        "g_final": _cols(a["norm_f"]), "g_mix2": _cols(a["mix_norm_2"][0]), "g_mlp2": _cols(a["mlp_norm_2"][0]),
        "b_qkv": _cols(bq), "b_in": _cols(a["a_b_in_2"][0]), "conv_b": _cols(a["a_conv_b_2"][0]),
        "ln_g": _cols(a["a_ln_g_2"][0]), "ln_b": _cols(a["a_ln_b_2"][0]), "b_out": _cols(a["a_b_out_2"][0]),
        "sinks": np.broadcast_to(a["attn_sinks"][0], (P, HEADS)), "glu": glu,
        "conv_w": a["a_conv_w_2"][0].reshape(TAPS, C, P).transpose(2, 1, 0).reshape(P, -1),
    }
    vec = np.ascontiguousarray(np.concatenate([parts[name] for name, _ in VEC_PARTS], axis=1))

    dist = np.arange(P)[:, None] + P - np.arange(2 * P)[None, :]
    near = np.where((dist >= 0) & (dist < P), -dist, MASKED).astype(np.float32)
    inv = np.broadcast_to((1.0 / np.arange(1, PAD + 1)).astype(np.float32), (P, PAD))
    cst = np.ascontiguousarray(np.concatenate([near, inv, np.eye(P, dtype=np.float32)], axis=1))

    arrays = {"xT": np.ascontiguousarray(a["x"][0].T.reshape(C, P, T).transpose(1, 0, 2)), "vec_in": vec, "cst_in": cst}
    arrays.update({f"w_{k}": t for k, t in w.items()})
    nc = _bacc.Bacc("TRN2", target_bir_lowering=False, num_devices=1)
    aps = {k: nc.dram_tensor(k, t.shape, F32, kind="ExternalInput").ap() for k, t in arrays.items()}
    out = nc.dram_tensor("outT", (P, C, T), F32, kind="ExternalOutput").ap()
    build(nc, aps["xT"], aps["vec_in"], aps["cst_in"], {k: aps[f"w_{k}"] for k in w}, out)
    r = _run(nc, [arrays], core_ids=[0])
    y = r.results[0]["outT"]
    return np.ascontiguousarray(y.transpose(1, 0, 2).reshape(D, T).T)[None]
```

```python
from contextlib import ExitStack

import numpy as np

import concourse.bass as bass
from concourse import mybir

F32 = mybir.dt.float32
F32R = mybir.dt.float32r
ALU = mybir.AluOpType
ACT = mybir.ActivationFunctionType
AX_X = mybir.AxisListType.X

P = 128
D = 1024
T = 512
C = D // P
NBLK = T // P
EPS = 1e-6
WINDOWS = (2, 4, 8, 16)
PAD = max(WINDOWS)
HEADS, KV, HD = 16, 4, 64
REP = HEADS // KV
FF_PAIRS = 2816 // P
FF_PARTS = (8, 8, 6)
MLP_PARTS = (8, 8, 8, 8)
TAPS = 31
PE_TAPS = (7,) * 7 + (13,)
POOL_TAPS = (11,) * 7 + (9,)
LATE_TAPS = (6,) * 7 + (0,)
PARTS = 6
SLOTS = 4
AHEAD = 3
KT = 8
MASKED = -1.0e30

VEC_PARTS = [("pool_b", C), ("pool_scale", C), ("g_mix0", C), ("g_mix1", C), ("g_ffn0", C), ("g_ffn1", C),
             ("g_final", C), ("g_mix2", C), ("g_mlp2", C), ("b_qkv", 12), ("b_in", 2 * C), ("conv_b", C),
             ("ln_g", C), ("ln_b", C), ("b_out", C), ("sinks", HEADS), ("glu", 2 * FF_PAIRS * 8),
             ("conv_w", C * TAPS)]
VEC = {}
_at = 0
for _name, _n in VEC_PARTS:
    VEC[_name] = _at
    _at += _n
VEC_COLS = _at
CST_DIST, CST_INV, CST_ID = 0, 2 * P, 2 * P + PAD
CST_COLS = CST_ID + P


class Phase:

    def __init__(self, name, weights, units, tiles, unit, chain):
        self.name, self.weights, self.units, self.tiles = name, weights, units, tiles
        self.unit, self.chain = unit, chain
        self.end_chain = chain + (2 * units if name == "pool" else units)


def plan(w):
    phases, unit, chain = {}, 0, 0

    def add(name, weights, units, tiles):
        nonlocal unit, chain
        phases[name] = ph = Phase(name, weights, units, tiles, unit, chain)
        unit, chain = unit + units, ph.end_chain

    def add_mlp(kind, parts, per_part):
        order = [("up", 0)]
        for q in range(1, len(parts)):
            order += [("up", q), ("down", q - 1)]
        order.append(("down", len(parts) - 1))
        for what, q in order:
            if what == "up":
                add(f"{kind}_up{q}", w[f"{kind}_up{q}"], per_part * parts[q], C)
            else:
                add(f"{kind}_down{q}", w[f"{kind}_down{q}"], C, parts[q])

    add("pool", w["pool"], 4, 4)
    add_mlp("ffn0", FF_PARTS, 2)
    add("qkv", w["qkv"], 12, C)
    add("wo", w["wo"], C, C)
    add_mlp("ffn1", FF_PARTS, 2)
    add("ain", w["ain"], 2 * C, C)
    add("aout", w["aout"], C, C)
    add_mlp("mlp", MLP_PARTS, 1)
    return phases, unit, chain


def row(t, c):
    if isinstance(c, int):
        return t[:, c, :]
    return t[:, bass.ds(c, 1), :].rearrange("p o n -> p (o n)")


def col(t, e):
    return t[:, e:e + 1] if isinstance(e, int) else t[:, bass.ds(e, 1)]


def run(eng, step, n, peel_first=False, peel_last=False):
    lo, hi = int(peel_first), n - int(peel_last)
    if peel_first:
        step(0)
    if hi - lo == 1:
        step(lo)
    elif hi > lo:
        with eng.Fori(lo, hi) as i:
            step(i)
    if peel_last:
        step(n - 1)


def build(nc, xT, vec_in, cst_in, w_in, out):
    ph, UNITS, CHAINS = plan(w_in)
    order = list(ph.values())

    with ExitStack() as ctx:
        def sb(name, shape, dt=F32, scope=ctx):
            return scope.enter_context(nc.sbuf_tensor(name, shape, dt))

        def sem(name):
            return ctx.enter_context(nc.semaphore(name))

        res = sb("res", [P, C, T])
        with ExitStack() as own:
            bias = sb("bias", [P, HEADS, 2 * P], F32, own)
        xh = sb("xh", [P, C, T], F32R)
        xl = sb("xl", [P, C, T], F32R)
        raw = sb("raw", [P, SLOTS, KT * P])
        whi = sb("whi", [P, SLOTS, KT * P], F32R)
        wlo = sb("wlo", [P, SLOTS, KT * P], F32R)
        vec = sb("vec", [P, VEC_COLS])
        cst = sb("cst", [P, CST_COLS])
        ones = sb("ones", [P, P])
        eps = sb("eps", [P, 2])
        gfm = sb("gfm", [P, C])
        r1 = sb("r1", [P, T])
        rms = sb("rms", [P, T])
        rinv = sb("rinv", [P, T])
        ssum = sb("ssum", [P, 2, T])
        sq = sb("sq", [P, 2, T])
        u = sb("u", [P, 4, 2 + T])
        tmp = sb("tmp", [P, 4, T])
        gate = sb("gate", [P, 2, T])
        prod = sb("prod", [P, 2, T])
        with ExitStack() as own:
            ahi = sb("ahi", [P, 2, 8, T], F32R, own)
            alo = sb("alo", [P, 2, 8, T], F32R, own)
        with ExitStack() as own:
            zp = sb("zp", [P, 3, 2, PAD + T], F32, own)
        with ExitStack() as own:
            ohi = sb("ohi", [P, C, T], F32R, own)
        with ExitStack() as own:
            qkvT = sb("qkvT", [P, 12, T], F32, own)
            olo = sb("olo", [P, C, T], F32R, own)
            vt = sb("vt", [P, NBLK, 2, P], F32, own)
            prob = sb("prob", [P, 3, REP, 2 * P], F32, own)
            pT = sb("pT", [P, 2, 2, REP * P], F32, own)
            oq = sb("oq", [P, 2, REP * HD], F32, own)
            stat = sb("stat", [P, 6, NBLK * KV, REP], F32, own)
        with ExitStack() as own:
            ylo = sb("ylo", [P, C, T], F32R, own)
            yhi = sb("yhi", [P, C, T], F32R, own)
        with ExitStack() as own:
            hv = sb("hv", [P, C, T], F32, own)
            hc = sb("hc", [P, 2, TAPS - 1 + T], F32, own)
            hch = sb("hch", [P, 2, TAPS - 1 + T], F32R, own)
            hcl = sb("hcl", [P, 2, TAPS - 1 + T], F32R, own)
            dgh = sb("dgh", [P, 2, max(PE_TAPS) * P], F32R, own)
            dgl = sb("dgl", [P, 2, max(PE_TAPS) * P], F32R, own)
            cwh = sb("cwh", [P, C * TAPS], F32R, own)
            cwl = sb("cwl", [P, C * TAPS], F32, own)
            tapped = sb("tapped", [P, PARTS, T], F32, own)
        bank = [ctx.enter_context(nc.psum_tensor(f"bank{b}", [P, T], F32)) for b in range(8)]
        acc = bank[0:4]
        norm = bank[4:6]
        taps = bank[5]

        x_in = [sem(f"x_in{q}") for q in range(4)]
        vec_loaded = sem("vec_loaded")
        cst_loaded = sem("cst_loaded")
        w_loaded = [sem(f"w_loaded{s}") for s in range(SLOTS)]
        hi_done = sem("hi_done")
        lo_done = sem("lo_done")
        chain_done = sem("chain_done")
        acc_free = sem("acc_free")
        setup = sem("setup")
        xh_ready = sem("xh_ready")
        xl_ready = sem("xl_ready")
        sq_ready = sem("sq_ready")
        ssum_ready = sem("ssum_ready")
        norm_done = sem("norm_done")
        rms_ready = sem("rms_ready")
        rinv_ready = sem("rinv_ready")
        slide = sem("slide")
        pooled = sem("pooled")
        tap2_done = sem("tap2_done")
        tap1_done = sem("tap1_done")
        tap0_done = sem("tap0_done")
        gate_ready = sem("gate_ready")
        prod_ready = sem("prod_ready")
        act_hi = sem("act_hi")
        act_lo = sem("act_lo")
        qkv_ready = sem("qkv_ready")
        vT_done = sem("vT_done")
        v_ready = sem("v_ready")
        scores_done = sem("scores_done")
        bias_ready = sem("bias_ready")
        biased = sem("biased")
        max_steps = sem("max_steps")
        exp_done = sem("exp_done")
        den_steps = sem("den_steps")
        pT_done = sem("pT_done")
        pT_ready = sem("pT_ready")
        pv_done = sem("pv_done")
        o_scaled = sem("o_scaled")
        oT_done = sem("oT_done")
        o_hi = sem("o_hi")
        o_lo = sem("o_lo")
        x2_ready = sem("x2_ready")
        sig_ready = sem("sig_ready")
        hc_ready = sem("hc_ready")
        hch_ready = sem("hch_ready")
        hcl_ready = sem("hcl_ready")
        taps_split = sem("taps_split")
        diag_ready = sem("diag_ready")
        conv_done = sem("conv_done")
        tapped_ready = sem("tapped_ready")
        tapped_steps = sem("tapped_steps")
        tap_steps = sem("tap_steps")
        late_steps = sem("late_steps")
        hv_ready = sem("hv_ready")
        mean_done = sem("mean_done")
        xc_ready = sem("xc_ready")
        xcsq_ready = sem("xcsq_ready")
        sqsum_done = sem("sqsum_done")
        ln_scaled = sem("ln_scaled")
        ln_silu = sem("ln_silu")
        ln_hi = sem("ln_hi")
        ln_lo = sem("ln_lo")
        stored = sem("stored")

        ident = cst[:, CST_ID:CST_ID + P]

        def v(name, e=0):
            return col(vec, VEC[name] + e)

        NORMS = ["pool", "ffn0", "qkv", "ffn1", "ain", "mlp"]
        GAIN = {"pool": "g_mix0", "ffn0": "g_ffn0", "qkv": "g_mix1", "ffn1": "g_ffn1", "mlp": "g_mlp2"}
        X = {name: C * k for k, name in enumerate(NORMS)}
        SS = {"qkv": 0, "ffn1": 9, "ain": 18, "mlp": 18 + 17}
        SQ = {"pool": 0, "ffn0": 8, "qkv": 16, "ffn1": 24, "ain": 32, "mlp": 48}
        ND = {"qkv": 0, "ffn1": 1, "ain": 2, "mlp": 4}
        RR = {"pool": 0, "ffn0": 1, "qkv": 2, "ffn1": 3, "ain": 4, "mlp": 7}

        pair0, act0 = {}, {}
        pairs = acts = 0
        for name in ph:
            kind, _, part = name.rpartition("_up")
            if kind.startswith("ffn"):
                pair0[name], act0[name] = pairs, acts
                pairs, acts = pairs + FF_PARTS[int(part)], acts + FF_PARTS[int(part)]
            elif kind == "mlp":
                act0[name] = acts
                acts += MLP_PARTS[int(part)]

        def used(unit):
            return 2 * unit + 2 if isinstance(unit, int) and unit < 4 else unit + 5

        def loads(base, i, k):
            return 16 * (i + (base + k) // SLOTS + 1)

        block = ctx.enter_context(nc.Block())

        @block.sync
        def _(sp):
            def load(p, i, k):
                unit = p.unit + SLOTS * i + k
                if isinstance(unit, int) and unit < SLOTS:
                    free, at = None, unit - p.unit
                elif isinstance(i, int):
                    free, at = unit - SLOTS + 1, SLOTS * i + k
                else:
                    free, at = sp.snap(unit - SLOTS + 1), sp.snap(SLOTS * i + k)
                src = p.weights[at] if isinstance(at, int) else \
                    p.weights[bass.ds(at, 1)].rearrange("o p n -> p (o n)")
                if free is not None:
                    sp.wait_ge(lo_done, free)
                sp.dma_start(raw[:, k, 0:p.tiles * P], src).then_inc(w_loaded[k], 16)

            for p in order:
                run(sp, lambda i: [load(p, i, k) for k in range(SLOTS)], p.units // SLOTS)
            last = ph["mlp_down3"]
            for c in range(C):
                sp.wait_ge(acc_free, last.chain + c + 1)
                sp.dma_start(out[:, c, :], res[:, c, :]).then_inc(stored, 16)
            sp.wait_ge(stored, 16 * C)

        @block.gpsimd
        def _(pool):
            pool.wait_ge(cst_loaded, 16)
            pool.wait_ge(chain_done, ph["qkv"].end_chain)
            for h in range(HEADS):
                slope = float(np.float32(2.0 ** (-8.0 / HEADS * (h + 1))))
                nc.gpsimd.tensor_scalar(bias[:, h, :], cst[:, CST_DIST:CST_DIST + 2 * P], slope * HD ** 0.5,
                                        None, ALU.mult).then_inc(bias_ready, 1)
            made = adds = 0
            for c in range(C):
                if c >= 2:
                    pool.wait_ge(hv_ready, c - 1)
                for k in range(1, POOL_TAPS[c]):
                    a = tapped[:, made % PARTS, :] if k == 1 else prod[:, c % 2, :]
                    pool.wait_ge(tapped_ready, made + k + 1)
                    if k > 1:
                        pool.wait_ge(tapped_steps, adds)
                    nc.gpsimd.tensor_tensor(prod[:, c % 2, :], a, tapped[:, (made + k) % PARTS, :], ALU.add)\
                        .then_inc(tapped_steps, 1)
                    adds += 1
                made += POOL_TAPS[c]

        @block.tensor
        def _(pe):
            def three(out_, hi, lo, mh, ml, first, last):
                nc.tensor.matmul(out_, hi, mh, start=first, stop=False)
                nc.tensor.matmul(out_, hi, ml, start=False, stop=False)
                return nc.tensor.matmul(out_, lo, mh, start=False, stop=last)

            def chain(p, i, k, hi, lo, count_x=None):
                chain_no = p.chain + SLOTS * i + k
                pe.wait_ge(lo_done, p.unit + SLOTS * i + k + 1)
                pe.wait_ge(acc_free, chain_no - 3)
                for t in range(p.tiles):
                    if count_x is not None:
                        pe.wait_ge(xl_ready, count_x + t + 1)
                    w = slice(t * P, (t + 1) * P)
                    mm = three(acc[k][:], whi[:, k, w], wlo[:, k, w], hi[:, t, :], lo[:, t, :],
                               t == 0, t == p.tiles - 1)
                mm.then_inc(chain_done, 1)

            def sum_features(name, which=0):
                adds = 17 if name == "ain" else 9
                pe.wait_ge(ssum_ready, SS[name] + adds)
                if which == 0:
                    pe.wait_ge(rms_ready, RR[name])
                nc.tensor.matmul(norm[which][:], ones[:], ssum[:, which, :], start=True, stop=True)\
                    .then_inc(norm_done, 1)

            def sum_squares(count):
                for c in range(C):
                    pe.wait_ge(sq_ready, count + c + 1)
                    mm = nc.tensor.matmul(norm[0][:], ones[:], sq[:, c % 2, :], start=(c == 0), stop=(c == C - 1))
                    mm.then_inc(sqsum_done, 1)

            def project(name, first):
                p = ph[name]

                def step(i):
                    peeled = first is not None and isinstance(i, int) and i == 0
                    for k in range(SLOTS):
                        chain(p, i, k, xh, xl, X[first] if peeled and k == 0 else None)
                        if peeled and k == 0 and first != "ffn0":
                            sum_features(first)
                run(pe, step, p.units // SLOTS, peel_first=first is not None)

            def down(name, buf, acts_before):
                p = ph[name]
                pe.wait_ge(act_lo, acts_before + p.tiles)
                run(pe, lambda i: [chain(p, i, k, ahi[:, buf], alo[:, buf]) for k in range(SLOTS)],
                    C // SLOTS)

            def feed_forward(kind, parts):
                for q in range(len(parts)):
                    project(f"{kind}_up{q}", kind if q == 0 else None)
                    if q:
                        down(f"{kind}_down{q - 1}", (q - 1) % 2, act0[f"{kind}_up{q - 1}"])
                q = len(parts) - 1
                down(f"{kind}_down{q}", q % 2, act0[f"{kind}_up{q}"])

            pe.wait_ge(setup, 1)
            sum_squares(SQ["pool"])
            for g in range(4):
                pe.wait_ge(lo_done, g + 1)
                for o in range(2):
                    c = 2 * g + o
                    if c >= 4:
                        pe.wait_ge(acc_free, c - 3)
                    for t in range(2):
                        pe.wait_ge(xl_ready, 2 * g + t + 1)
                        w = slice((2 * o + t) * P, (2 * o + t + 1) * P)
                        mm = three(acc[c % 4][:], whi[:, g, w], wlo[:, g, w], xh[:, 2 * g + t, :],
                                   xl[:, 2 * g + t, :], t == 0, t == 1)
                    mm.then_inc(chain_done, 1)
            pe.wait_ge(rms_ready, 1)
            sum_squares(SQ["ffn0"])

            feed_forward("ffn0", FF_PARTS)

            project("qkv", "qkv")
            pe.wait_ge(qkv_ready, 12)
            pe.wait_ge(cst_loaded, 16)
            for pr in range(2):
                for n in range(NBLK):
                    mm = nc.tensor.transpose(bank[6 + pr][:, n * P:(n + 1) * P],
                                             qkvT[:, 10 + pr, n * P:(n + 1) * P], ident)
                mm.then_inc(vT_done, 1)

            STEPS = [(n, g) for n in range(NBLK) for g in range(KV)]

            def keys(n):
                return P if n == 0 else 0

            def scores(s):
                n, g = STEPS[s]
                k0, half = keys(n), slice(HD * (g % 2), HD * (g % 2) + HD)
                if s >= 2:
                    pe.wait_ge(biased, REP * (s - 1))
                for i in range(REP):
                    o = (i % 2) * 2 * P
                    mm = nc.tensor.matmul(acc[2 * (s % 2) + i // 2][:, o + k0:o + 2 * P],
                                          qkvT[half, 4 * (g // 2) + i, n * P:(n + 1) * P],
                                          qkvT[half, 8 + g // 2, (n - 1) * P + k0:(n + 1) * P],
                                          start=True, stop=True)
                mm.then_inc(scores_done, 1)

            def transposes(s):
                n, _ = STEPS[s]
                pe.wait_ge(exp_done, s + 1)
                if s >= 1:
                    pe.wait_ge(pT_ready, s)
                for b in range(keys(n) // P, 2):
                    for i in range(REP):
                        mm = nc.tensor.transpose(bank[4 + b][:, i * P:(i + 1) * P],
                                                 prob[:, s % 3, i, b * P:(b + 1) * P], ident)
                mm.then_inc(pT_done, 1)

            def values(s):
                n, g = STEPS[s]
                pe.wait_ge(pT_ready, s + 1)
                if s == 0:
                    pe.wait_ge(v_ready, 2)
                else:
                    pe.wait_ge(o_scaled, s)
                half = slice(HD * (g % 2), HD * (g % 2) + HD)
                b0 = keys(n) // P
                for i in range(REP):
                    for b in range(b0, 2):
                        mm = nc.tensor.matmul(bank[6][:, i * HD:(i + 1) * HD], pT[:, s % 2, b, i * P:(i + 1) * P],
                                              vt[:, n - 1 + b, g // 2, half], start=(b == b0), stop=(b == 1))
                mm.then_inc(pv_done, 1)

            def out_transposes(s):
                pe.wait_ge(o_scaled, s + 1)
                if s == 0:
                    pe.wait_ge(v_ready, 2)
                else:
                    pe.wait_ge(o_lo, s)
                for j in range(2):
                    mm = nc.tensor.transpose(bank[7][:, j * P:(j + 1) * P], oq[:, s % 2, j * P:(j + 1) * P], ident)
                mm.then_inc(oT_done, 1)

            last = len(STEPS) - 1
            scores(0)
            scores(1)
            for s in range(last + 3):
                if s + 2 <= last:
                    scores(s + 2)
                if s <= last:
                    transposes(s)
                if 1 <= s <= last + 1:
                    values(s - 1)
                if s >= 2:
                    out_transposes(s - 2)

            pe.wait_ge(o_lo, len(STEPS))
            pe.wait_ge(biased, REP * len(STEPS))
            p = ph["wo"]
            run(pe, lambda i: [chain(p, i, k, ohi, olo) for k in range(SLOTS)], p.units // SLOTS)

            feed_forward("ffn1", FF_PARTS)

            p = ph["ain"]

            def convolve(c):
                b = c % 2
                pe.wait_ge(hcl_ready, c + 1)
                pe.wait_ge(diag_ready, c + 1)
                if c >= 2:
                    pe.wait_ge(hv_ready, c - 1)
                for k in range(PE_TAPS[c]):
                    w = slice(k * P, (k + 1) * P)
                    mm = three(bank[6 + b][:], dgh[:, b, w], dgl[:, b, w], hch[:, b, k:k + T],
                               hcl[:, b, k:k + T], k == 0, k == PE_TAPS[c] - 1)
                mm.then_inc(conv_done, 1)

            def feature_sum(c):
                if c == 0:
                    pe.wait_ge(rms_ready, RR["ain"] + 2)
                pe.wait_ge(hv_ready, c + 1)
                mm = nc.tensor.matmul(norm[0][:], ones[:], hv[:, c, :], start=(c == 0), stop=(c == C - 1))
                if c == C - 1:
                    mm.then_inc(mean_done, 1)

            for c in range(C):
                for k in (2 * (c % 2), 2 * (c % 2) + 1):
                    chain(p, c // 2, k, xh, xl, X["ain"] if c == 0 and k == 0 else None)
                    if c == 0 and k == 0:
                        sum_features("ain")
                        sum_features("ain", 1)
                if c >= 1:
                    convolve(c - 1)
                if c >= 2:
                    feature_sum(c - 2)
            convolve(C - 1)
            feature_sum(C - 2)
            feature_sum(C - 1)
            for c in range(C):
                pe.wait_ge(xcsq_ready, c + 1)
                mm = nc.tensor.matmul(norm[1][:], ones[:], sq[:, c % 2, :], start=(c == 0), stop=(c == C - 1))
                mm.then_inc(sqsum_done, 1)
            p = ph["aout"]
            for k in range(p.units):
                pe.wait_ge(lo_done, p.unit + k + 1)
                pe.wait_ge(acc_free, p.chain + k - 3)
                for t in range(C):
                    if k == 0:
                        pe.wait_ge(ln_lo, t + 1)
                    w = slice(t * P, (t + 1) * P)
                    mm = three(acc[k % 4][:], whi[:, k % 4, w], wlo[:, k % 4, w], yhi[:, t, :], ylo[:, t, :],
                               t == 0, t == C - 1)
                mm.then_inc(chain_done, 1)

            feed_forward("mlp", MLP_PARTS)

        @block.scalar
        def _(act):
            def split_hi(base, i, k, tiles=KT):
                if isinstance(i, int) and base + SLOTS * i + k >= UNITS:
                    return
                s, unit = k % SLOTS, base + SLOTS * i + k
                act.wait_ge(w_loaded[s], loads(base, i, k))
                if not (isinstance(unit, int) and unit < SLOTS):
                    act.wait_ge(chain_done, used(unit - SLOTS))
                nc.scalar.activation(whi[:, s, 0:tiles * P], raw[:, s, 0:tiles * P], ACT.Copy)\
                    .then_inc(hi_done, 1)

            def prepare(name, c, buf, reads_done):
                if name == "ain":
                    gain = col(gfm, c)
                else:
                    gain = v(GAIN[name], c)
                if reads_done:
                    act.wait_ge(chain_done, reads_done)
                nc.scalar.activation(row(xh, c), row(res, c), ACT.Copy, scale=gain).then_inc(xh_ready, 1)
                if name == "ain":
                    nc.scalar.activation(sq[:, 0, :], row(res, c), ACT.Square).then_inc(sq_ready, 1)
                    nc.scalar.activation(sq[:, 1, :], row(res, c), ACT.Square, scale=v("g_final", c))\
                        .then_inc(sq_ready, 1)
                else:
                    nc.scalar.activation(sq[:, buf, :], row(res, c), ACT.Square).then_inc(sq_ready, 1)

            def root(name, which=0):
                if name == "ffn0":
                    act.wait_ge(sqsum_done, 2 * C)
                else:
                    act.wait_ge(norm_done, ND[name] + 1)
                nc.scalar.activation(rms[:], norm[which][:], ACT.Sqrt, scale=1.0 / D, bias=eps[:, 0:1])\
                    .then_inc(rms_ready, 1)

            def finish(name, norm_name, reads_done):
                p = ph[name]

                def step(i):
                    for k in range(SLOTS):
                        split_hi(p.unit, i, k + AHEAD)
                        act.wait_ge(acc_free, p.chain + SLOTS * i + k + 1)
                        prepare(norm_name, SLOTS * i + k, k % 2, reads_done)
                run(act, step, C // SLOTS)

            def plain(name, peel_last=False):
                p = ph[name]
                run(act, lambda i: [split_hi(p.unit, i, k + AHEAD) for k in range(SLOTS)], p.units // SLOTS,
                    peel_last=peel_last)

            def ffn_up(name, layer, buf, first, buffer_free):
                p = ph[name]
                pair_base, act_base, q0 = pair0[name], act0[name], pair0[name] % FF_PAIRS

                def step(i):
                    for b in range(2):
                        pair = pair_base + 2 * i + b
                        for j in range(2):
                            k = 2 * b + j
                            split_hi(p.unit, i, k + AHEAD)
                            if first and isinstance(i, int) and i == 0 and k == 0:
                                root(first)
                            par = VEC["glu"] + ((layer * FF_PAIRS + q0) * 2 + k) * 4 + 16 * i
                            act.wait_ge(acc_free, p.chain + SLOTS * i + k + 1)
                            act.wait_ge(vec_loaded, 16)
                            nc.scalar.activation(tmp[:, k, :], u[:, k, 2:2 + T], ACT.Identity,
                                                 scale=col(vec, par + 2), bias=col(vec, par + 3))\
                                .then_inc(tap2_done, 1)
                        act.wait_ge(tap0_done, 2 * pair + 2)
                        nc.scalar.activation(gate[:, b, :], tmp[:, 2 * b + 1, :], ACT.Silu)\
                            .then_inc(gate_ready, 1)
                        act.wait_ge(prod_ready, act_base + 2 * i + b + 1)
                        act.wait_ge(chain_done, buffer_free)
                        nc.scalar.activation(row(ahi[:, buf], 2 * i + b), prod[:, b, :], ACT.Copy)\
                            .then_inc(act_hi, 1)
                run(act, step, p.units // SLOTS, peel_first=bool(first))

            def mlp_up(name, buf, first, buffer_free):
                p, act_base = ph[name], act0[name]

                def step(i):
                    for k in range(SLOTS):
                        split_hi(p.unit, i, k + AHEAD)
                        if first and isinstance(i, int) and i == 0 and k == 0:
                            root(first)
                        act.wait_ge(prod_ready, act_base + SLOTS * i + k + 1)
                        act.wait_ge(chain_done, buffer_free)
                        nc.scalar.activation(row(ahi[:, buf], SLOTS * i + k), tmp[:, k, :], ACT.Copy)\
                            .then_inc(act_hi, 1)
                run(act, step, p.units // SLOTS, peel_first=bool(first))

            def feed_forward(kind, parts, layer, next_norm):
                n = len(parts)
                for q in range(n):
                    up = f"{kind}_up{q}"
                    free = ph[f"{kind}_down{q - 2}"].end_chain if q >= 2 else ph[up].chain
                    if kind == "mlp":
                        mlp_up(up, q % 2, kind if q == 0 else None, free)
                    else:
                        ffn_up(up, layer, q % 2, kind if q == 0 else None, free)
                    if q:
                        plain(f"{kind}_down{q - 1}")
                if next_norm:
                    finish(f"{kind}_down{n - 1}", next_norm, ph[f"{kind}_up{n - 1}"].end_chain)
                else:
                    plain(f"{kind}_down{n - 1}", peel_last=True)

            act.dma_start(vec[:], vec_in).then_inc(vec_loaded, 16)
            for q in range(4):
                act.dma_start(res[:, 2 * q:2 * q + 2, :], xT[:, 2 * q:2 * q + 2, :]).then_inc(x_in[q], 16)
            act.dma_start(cst[:], cst_in).then_inc(cst_loaded, 16)

            act.wait_ge(setup, 2)
            act.wait_ge(vec_loaded, 16)
            for c in range(C):
                if c % 2 == 0:
                    act.wait_ge(x_in[c // 2], 16)
                if c >= 2:
                    act.wait_ge(sqsum_done, c - 1)
                prepare("pool", c, c % 2, 0)
                if c in (1, 3, 5):
                    split_hi(0, 0, c // 2, 4)
            act.wait_ge(sqsum_done, C)
            nc.scalar.activation(rms[:], norm[0][:], ACT.Sqrt, scale=1.0 / D, bias=eps[:, 0:1]).then_inc(rms_ready, 1)
            for c in range(C):
                if c % 2 == 0:
                    split_hi(0, 0, c // 2 + AHEAD, 4 if c == 0 else KT)
                act.wait_ge(pooled, c + 1)
                if c >= 2:
                    act.wait_ge(sqsum_done, C + c - 1)
                prepare("ffn0", c, c % 2, 2 * (c // 2) + 2)

            feed_forward("ffn0", FF_PARTS, 0, "qkv")

            p = ph["qkv"]

            def qkv_step(i):
                for k in range(SLOTS):
                    split_hi(p.unit, i, k + AHEAD)
                    if isinstance(i, int) and k == 0:
                        root("qkv")
                    m = SLOTS * i + k
                    act.wait_ge(acc_free, p.chain + m + 1)
                    act.wait_ge(vec_loaded, 16)
                    nc.scalar.activation(row(qkvT, m), tmp[:, k, :], ACT.Identity, bias=v("b_qkv", m))\
                        .then_inc(qkv_ready, 1)
            run(act, qkv_step, 3, peel_first=True)
            for pr in range(2):
                act.wait_ge(vT_done, pr + 1)
                nc.scalar.activation(vt[:, :, pr, :], bank[6 + pr][:].rearrange("p (n d) -> p n d", n=NBLK),
                                     ACT.Copy).then_inc(v_ready, 1)

            def exps(s):
                k0 = P if s // KV == 0 else 0
                act.wait_ge(max_steps, 2 * (s + 1))
                for i in range(REP):
                    a = prob[:, s % 3, i, k0:2 * P]
                    nc.scalar.activation(a, a, ACT.Exp, bias=stat[:, 1, s, i:i + 1],
                                         accum_out=stat[:, 3, s, i:i + 1])
                nc.scalar.activation(stat[:, 4, s, :], stat[:, 2, s, :], ACT.Exp).then_inc(exp_done, 1)

            def copy_pT(s):
                b0 = 1 if s // KV == 0 else 0
                act.wait_ge(pT_done, s + 1)
                if s >= 2:
                    act.wait_ge(pv_done, s - 1)
                for b in range(b0, 2):
                    last = nc.scalar.activation(pT[:, s % 2, b, :], bank[4 + b][:], ACT.Copy)
                last.then_inc(pT_ready, 1)

            def out_hi(s):
                n, g = s // KV, s % KV
                act.wait_ge(oT_done, s + 1)
                nc.scalar.activation(ohi[:, 2 * g:2 * g + 2, n * P:(n + 1) * P],
                                     bank[7][:, 0:2 * P].rearrange("p (j q) -> p j q", j=2), ACT.Copy)\
                    .then_inc(o_hi, 1)

            last = NBLK * KV - 1
            exps(0)
            for s in range(last + 4):
                if s >= 3:
                    out_hi(s - 3)
                if s + 1 <= last:
                    exps(s + 1)
                if s <= last:
                    copy_pT(s)
            finish("wo", "ffn1", ph["qkv"].end_chain)

            feed_forward("ffn1", FF_PARTS, 1, "ain")

            nc.scalar.activation(cwh[:], vec[:, VEC["conv_w"]:VEC["conv_w"] + C * TAPS], ACT.Copy)\
                .then_inc(taps_split, 1)
            p = ph["ain"]

            def diagonals(c):
                if c >= 2:
                    act.wait_ge(conv_done, c - 1)
                for k in range(PE_TAPS[c]):
                    e = c * TAPS + k
                    nc.scalar.activation(dgh[:, c % 2, k * P:(k + 1) * P], ident, ACT.Copy,
                                         scale=cwh[:, e:e + 1].bitcast(F32))
                    last = nc.scalar.activation(dgl[:, c % 2, k * P:(k + 1) * P], ident, ACT.Copy,
                                                scale=cwl[:, e:e + 1])
                last.then_inc(diag_ready, 1)

            def products(c, ks):
                for k in ks:
                    n = sum(POOL_TAPS[:c]) + k
                    if n >= PARTS:
                        m = n - PARTS
                        cm = next(j for j in range(C) if m < sum(POOL_TAPS[:j + 1]))
                        act.wait_ge(tapped_steps, sum(POOL_TAPS[:cm]) - cm + max(m - sum(POOL_TAPS[:cm]), 1))
                    tap = PE_TAPS[c] + k
                    nc.scalar.activation(tapped[:, n % PARTS, :], hc[:, c % 2, tap:tap + T], ACT.Identity,
                                         scale=v("conv_w", c * TAPS + tap),
                                         bias=v("conv_b", c) if k == 0 else 0.0).then_inc(tapped_ready, 1)

            act.wait_ge(taps_split, 2)
            diagonals(0)
            for c in range(C):
                for j in range(2):
                    split_hi(p.unit, 0, 2 * c + j + AHEAD)
                    if c == 0 and j == 0:
                        act.wait_ge(rinv_ready, 6)
                        nc.scalar.activation(rms[:], rinv[:], ACT.Sqrt, scale=1.0 / D, bias=eps[:, 1:2])\
                            .then_inc(rms_ready, 1)
                        nc.scalar.activation(r1[:], norm[0][:], ACT.Sqrt, scale=1.0 / D, bias=eps[:, 0:1])\
                            .then_inc(rms_ready, 1)
                if c >= 1:
                    products(c - 1, range(PARTS, POOL_TAPS[c - 1]))
                act.wait_ge(acc_free, p.chain + 2 * c + 2)
                nc.scalar.activation(gate[:, c % 2, :], tmp[:, 2 * (c % 2) + 1, :], ACT.Sigmoid,
                                     bias=v("b_in", C + c)).then_inc(sig_ready, 1)
                act.wait_ge(hc_ready, c + 2)
                if c >= 2:
                    act.wait_ge(conv_done, c - 1)
                nc.scalar.activation(hch[:, c % 2, :], hc[:, c % 2, :], ACT.Copy).then_inc(hch_ready, 1)
                products(c, range(PARTS))
                if c + 1 < C:
                    diagonals(c + 1)
            products(C - 1, range(PARTS, POOL_TAPS[C - 1]))
            for c in range(C):
                act.wait_ge(xc_ready, c + 1)
                if c >= 2:
                    act.wait_ge(sqsum_done, 2 * C + c - 1)
                nc.scalar.activation(sq[:, c % 2, :], hv[:, c, :], ACT.Square).then_inc(xcsq_ready, 1)
            act.wait_ge(sqsum_done, 3 * C)
            nc.scalar.activation(rms[:], norm[1][:], ACT.Sqrt, scale=1.0 / D, bias=eps[:, 0:1]).then_inc(rms_ready, 1)
            for c in range(C):
                act.wait_ge(ln_scaled, c + 1)
                nc.scalar.activation(hv[:, c, :], hv[:, c, :], ACT.Silu, scale=v("ln_g", c), bias=v("ln_b", c))\
                    .then_inc(ln_silu, 1)
                act.wait_ge(ln_silu, c + 1)
                nc.scalar.activation(yhi[:, c, :], hv[:, c, :], ACT.Copy).then_inc(ln_hi, 1)
            finish("aout", "mlp", ph["ain"].end_chain)

            feed_forward("mlp", MLP_PARTS, None, None)

        @block.vector
        def _(dve):
            V = nc.vector

            def split_lo(base, i, k, tiles=KT):
                if isinstance(i, int) and base + SLOTS * i + k >= UNITS:
                    return
                s = k % SLOTS
                dve.wait_ge(hi_done, base + SLOTS * i + k + 1)
                V.tensor_tensor(wlo[:, s, 0:tiles * P], raw[:, s, 0:tiles * P],
                                whi[:, s, 0:tiles * P].bitcast(F32), ALU.subtract).then_inc(lo_done, 1)

            def prepare(name, c, buf, reads=True):
                gain = col(gfm, c) if name == "ain" else v(GAIN[name], c)
                dve.wait_ge(xh_ready, X[name] + c + 1)
                V.scalar_tensor_tensor(row(xl, c), row(res, c), gain, row(xh, c).bitcast(F32),
                                       op0=ALU.mult, op1=ALU.subtract).then_inc(xl_ready, 1)
                if name in ("pool", "ffn0"):
                    return
                for which in range(2 if name == "ain" else 1):
                    per = 2 if name == "ain" else 1
                    src = which if name == "ain" else buf
                    dve.wait_ge(sq_ready, SQ[name] + per * c + which + 1)
                    dve.wait_ge(ssum_ready, SS[name] + per * c + which + 1)
                    V.tensor_tensor(ssum[:, which, :], ssum[:, which, :], sq[:, src, :], ALU.add)\
                        .then_inc(ssum_ready, 1)

            def invert(name, k0):
                dve.wait_ge(rms_ready, RR[name] + 1)
                V.reciprocal(rinv[:], rms[:]).then_inc(rinv_ready, 1)
                if name in SS:
                    V.memset(ssum[:], 0.0).then_inc(ssum_ready, 1)
                dve.wait_ge(rinv_ready, k0)

            def add_residual(p, i, k):
                c = SLOTS * i + k
                dve.wait_ge(chain_done, p.chain + c + 1)
                V.tensor_tensor(row(res, c), acc[k][:], row(res, c), ALU.add).then_inc(acc_free, 1)

            def finish(name, norm_name, out_bias=None):
                p = ph[name]

                def step(i):
                    for k in range(SLOTS):
                        c = SLOTS * i + k
                        split_lo(p.unit, i, k + AHEAD)
                        if out_bias:
                            V.scalar_tensor_tensor(row(res, c), row(res, c), v("g_final", c), r1[:],
                                                   op0=ALU.mult, op1=ALU.mult).then_inc(x2_ready, 1)
                            dve.wait_ge(x2_ready, c + 1)
                            dve.wait_ge(chain_done, p.chain + c + 1)
                            V.scalar_tensor_tensor(row(res, c), acc[k][:], v(out_bias, c), row(res, c),
                                                   op0=ALU.add, op1=ALU.add).then_inc(acc_free, 1)
                        else:
                            add_residual(p, i, k)
                        prepare(norm_name, c, k % 2)
                run(dve, step, C // SLOTS)

            def plain_down(name, peel_last=False):
                p = ph[name]

                def step(i):
                    for k in range(SLOTS):
                        split_lo(p.unit, i, k + AHEAD)
                        add_residual(p, i, k)
                run(dve, step, C // SLOTS, peel_last=peel_last)

            def ffn_up(name, layer, buf, first, rinv_count):
                p = ph[name]
                pair_base, act_base, q0 = pair0[name], act0[name], pair0[name] % FF_PAIRS

                def step(i):
                    for b in range(2):
                        pair = pair_base + 2 * i + b
                        par = VEC["glu"] + ((layer * FF_PAIRS + q0) * 2 + 2 * b) * 4 + 16 * i
                        split_lo(p.unit, i, 2 * b + AHEAD)
                        if first and isinstance(i, int) and i == 0 and b == 0:
                            invert(first, rinv_count)
                        for j in range(2):
                            k = 2 * b + j
                            dve.wait_ge(chain_done, p.chain + SLOTS * i + k + 1)
                            V.tensor_tensor(u[:, k, 2:2 + T], acc[k][:], rinv[:], ALU.mult).then_inc(acc_free, 1)
                        for shift, done, before in ((1, tap1_done, tap2_done), (0, tap0_done, tap1_done)):
                            for j in range(2):
                                k = 2 * b + j
                                dve.wait_ge(before, 2 * pair + j + 1)
                                V.scalar_tensor_tensor(tmp[:, k, :], u[:, k, shift:shift + T],
                                                       col(vec, par + 4 * j + shift), tmp[:, k, :],
                                                       op0=ALU.mult, op1=ALU.add).then_inc(done, 1)
                        split_lo(p.unit, i, 2 * b + 1 + AHEAD)
                        dve.wait_ge(gate_ready, pair + 1)
                        V.tensor_tensor(prod[:, b, :], tmp[:, 2 * b, :], gate[:, b, :], ALU.mult)\
                            .then_inc(prod_ready, 1)
                        dve.wait_ge(act_hi, act_base + 2 * i + b + 1)
                        V.tensor_tensor(row(alo[:, buf], 2 * i + b), prod[:, b, :],
                                        row(ahi[:, buf], 2 * i + b).bitcast(F32), ALU.subtract)\
                            .then_inc(act_lo, 1)
                run(dve, step, p.units // SLOTS, peel_first=bool(first))

            def mlp_up(name, buf, first, rinv_count):
                p, act_base = ph[name], act0[name]

                def step(i):
                    for k in range(SLOTS):
                        split_lo(p.unit, i, k + AHEAD)
                        if first and isinstance(i, int) and i == 0 and k == 0:
                            invert(first, rinv_count)
                        a = act_base + SLOTS * i + k
                        dve.wait_ge(chain_done, p.chain + SLOTS * i + k + 1)
                        V.tensor_tensor(u[:, k, 2:2 + T], acc[k][:], rinv[:], ALU.mult).then_inc(acc_free, 1)
                        dve.wait_ge(acc_free, p.chain + SLOTS * i + k + 1)
                        V.scalar_tensor_tensor(tmp[:, k, :], u[:, k, 2:2 + T], 0.0, u[:, k, 2:2 + T],
                                               op0=ALU.max, op1=ALU.mult).then_inc(prod_ready, 1)
                        dve.wait_ge(act_hi, a + 1)
                        V.tensor_tensor(row(alo[:, buf], SLOTS * i + k), tmp[:, k, :],
                                        row(ahi[:, buf], SLOTS * i + k).bitcast(F32), ALU.subtract)\
                            .then_inc(act_lo, 1)
                run(dve, step, p.units // SLOTS, peel_first=bool(first))

            def feed_forward(kind, parts, layer, next_norm, rinv_count):
                n = len(parts)
                for q in range(n):
                    if kind == "mlp":
                        mlp_up(f"{kind}_up{q}", q % 2, kind if q == 0 else None, rinv_count)
                    else:
                        ffn_up(f"{kind}_up{q}", layer, q % 2, kind if q == 0 else None, rinv_count)
                    if q:
                        plain_down(f"{kind}_down{q - 1}")
                if next_norm:
                    finish(f"{kind}_down{n - 1}", next_norm)
                else:
                    plain_down(f"{kind}_down{n - 1}", peel_last=True)

            V.memset(ones[:], 1.0)
            V.memset(eps[:, 0:1], EPS)
            V.memset(eps[:, 1:2], EPS * EPS)
            V.memset(u[:, :, 0:2], 0.0)
            V.memset(zp[:, :, :, 0:PAD], 0.0).then_inc(setup, 1)
            V.memset(ssum[:], 0.0).then_inc(ssum_ready, 1)
            dve.wait_ge(vec_loaded, 16)
            V.tensor_tensor(gfm[:], vec[:, VEC["g_final"]:VEC["g_final"] + C],
                            vec[:, VEC["g_mix2"]:VEC["g_mix2"] + C], ALU.mult).then_inc(setup, 1)

            for c in range(C):
                prepare("pool", c, c % 2)
                if c in (1, 3, 5):
                    split_lo(0, 0, c // 2, 4)
            invert("pool", 1)
            dve.wait_ge(cst_loaded, 16)
            steps = 0

            def stepped(ins):
                nonlocal steps
                steps += 1
                ins.then_inc(slide, 1)
                dve.wait_ge(slide, steps)

            tok = slice(PAD, PAD + T)
            for g, win in enumerate(WINDOWS):
                split_lo(0, 0, g + AHEAD, 4 if g == 0 else KT)
                z, y = zp[:, 0], tmp[:, 2 * (g % 2):2 * (g % 2) + 2, :]
                for o in range(2):
                    c = 2 * g + o
                    dve.wait_ge(chain_done, c + 1)
                    V.tensor_tensor(z[:, o, tok], acc[c % 4][:], rinv[:], ALU.mult).then_inc(acc_free, 1)
                dve.wait_ge(acc_free, 2 * g + 2)
                src, shift, dst = z, 1, 1
                while shift < win:
                    stepped(V.tensor_tensor(zp[:, dst, :, tok], src[:, :, tok],
                                            src[:, :, PAD - shift:PAD - shift + T], ALU.add))
                    src, shift, dst = zp[:, dst], 2 * shift, 3 - dst
                e = win - 1
                inv = cst[:, CST_INV:CST_INV + e]
                for o in range(2):
                    V.tensor_tensor(prod[:, o, 0:e], src[:, o, PAD:PAD + e], inv, ALU.mult)
                stepped(V.scalar_tensor_tensor(y, src[:, :, tok], 1.0 / win, z[:, :, tok],
                                               op0=ALU.mult, op1=ALU.subtract))
                stepped(V.tensor_tensor(y[:, :, 0:e], prod[:, :, 0:e], z[:, :, PAD:PAD + e], ALU.subtract))
                for o in range(2):
                    c = 2 * g + o
                    last_step = V.tensor_scalar(y[:, o, :], y[:, o, :], v("pool_b", c), v("pool_scale", c),
                                                ALU.add, ALU.mult)
                stepped(last_step)
                for o in range(2):
                    c = 2 * g + o
                    V.tensor_tensor(res[:, c, :], res[:, c, :], y[:, o, :], ALU.add).then_inc(pooled, 1)
                dve.wait_ge(pooled, 2 * g + 2)
                for o in range(2):
                    prepare("ffn0", 2 * g + o, o)

            feed_forward("ffn0", FF_PARTS, 0, "qkv", 2)

            p = ph["qkv"]

            def qkv_step(i):
                for k in range(SLOTS):
                    split_lo(p.unit, i, k + AHEAD)
                    if isinstance(i, int) and k == 0:
                        invert("qkv", 3)
                    dve.wait_ge(chain_done, p.chain + SLOTS * i + k + 1)
                    if not isinstance(i, int):
                        dve.wait_ge(qkv_ready, SLOTS * i + k - 3)
                    V.tensor_tensor(tmp[:, k, :], acc[k][:], rinv[:], ALU.mult).then_inc(acc_free, 1)
            run(dve, qkv_step, 3, peel_first=True)

            def front(s):
                k0, g = P if s // KV == 0 else 0, s % KV
                dve.wait_ge(scores_done, s + 1)
                dve.wait_ge(bias_ready, REP * (g + 1))
                if s >= 3:
                    dve.wait_ge(pT_done, s - 2)
                for i in range(REP):
                    o, h = (i % 2) * 2 * P, REP * g + i
                    V.tensor_tensor_reduce(out=prob[:, s % 3, i, k0:2 * P],
                                           in0=acc[2 * (s % 2) + i // 2][:, o + k0:o + 2 * P],
                                           in1=bias[:, h, k0:2 * P], scale=HD ** -0.5, scalar=v("sinks", h),
                                           op0=ALU.add, op1=ALU.max, accum_out=stat[:, 0, s, i:i + 1])\
                        .then_inc(biased, 1)
                dve.wait_ge(biased, REP * (s + 1))
                V.tensor_scalar(stat[:, 1, s, :], stat[:, 0, s, :], -1.0, None, ALU.mult).then_inc(max_steps, 1)
                V.tensor_tensor(stat[:, 2, s, :], vec[:, VEC["sinks"] + REP * g:VEC["sinks"] + REP * (g + 1)],
                                stat[:, 0, s, :], ALU.subtract).then_inc(max_steps, 1)

            def out_scale(s):
                dve.wait_ge(exp_done, s + 1)
                V.tensor_tensor(stat[:, 4, s, :], stat[:, 3, s, :], stat[:, 4, s, :], ALU.add).then_inc(den_steps, 1)
                dve.wait_ge(den_steps, 2 * s + 1)
                V.reciprocal(stat[:, 5, s, :], stat[:, 4, s, :]).then_inc(den_steps, 1)
                dve.wait_ge(den_steps, 2 * s + 2)
                dve.wait_ge(pv_done, s + 1)
                if s >= 2:
                    dve.wait_ge(oT_done, s - 1)
                V.tensor_tensor(oq[:, s % 2, :].rearrange("p (i d) -> p i d", i=REP),
                                bank[6][:, 0:REP * HD].rearrange("p (i d) -> p i d", i=REP),
                                stat[:, 5, s, :].rearrange("p (i o) -> p i o", o=1).broadcast_to([P, REP, HD]),
                                ALU.mult).then_inc(o_scaled, 1)

            def out_lo(s):
                n, g = s // KV, s % KV
                at = (slice(None), slice(2 * g, 2 * g + 2), slice(n * P, (n + 1) * P))
                dve.wait_ge(o_hi, s + 1)
                V.tensor_tensor(olo[at], bank[7][:, 0:2 * P].rearrange("p (j q) -> p j q", j=2),
                                ohi[at].bitcast(F32), ALU.subtract).then_inc(o_lo, 1)

            last = NBLK * KV - 1
            front(0)
            front(1)
            for s in range(last + 4):
                if 2 <= s <= last + 2:
                    out_scale(s - 2)
                if s >= 3:
                    out_lo(s - 3)
                if s + 2 <= last:
                    front(s + 2)
            finish("wo", "ffn1")

            feed_forward("ffn1", FF_PARTS, 1, "ain", 4)

            p = ph["ain"]
            dve.wait_ge(taps_split, 1)
            V.tensor_tensor(cwl[:], vec[:, VEC["conv_w"]:VEC["conv_w"] + C * TAPS], cwh[:].bitcast(F32),
                            ALU.subtract).then_inc(taps_split, 1)
            V.memset(hc[:, :, 0:TAPS - 1], 0.0).then_inc(hc_ready, 1)
            LATE_START = 2

            def own_taps(c):
                return range(PE_TAPS[c] + POOL_TAPS[c], TAPS - LATE_TAPS[c])

            def late_taps(c):
                return range(TAPS - LATE_TAPS[c], TAPS)

            def own_tap(c, n, k):
                x, w = hc[:, c % 2, k:k + T], v("conv_w", c * TAPS + k)
                if n == 0:
                    V.tensor_scalar(taps[:], x, w, None, ALU.mult).then_inc(tap_steps, 1)
                    return
                dve.wait_ge(tap_steps, sum(len(own_taps(j)) for j in range(c)) + n)
                V.scalar_tensor_tensor(hv[:, c, :] if n == len(own_taps(c)) - 1 else taps[:], x, w, taps[:],
                                       op0=ALU.mult, op1=ALU.add).then_inc(tap_steps, 1)

            def late_tap(c, n, k):
                x, w, at = hc[:, c % 2, k:k + T], v("conv_w", c * TAPS + k), bank[6 + c % 2][:]
                if n == 0:
                    dve.wait_ge(conv_done, c + 1)
                else:
                    dve.wait_ge(late_steps, sum(LATE_TAPS[:c]) + c + n)
                V.scalar_tensor_tensor(at, x, w, at, op0=ALU.mult, op1=ALU.add).then_inc(late_steps, 1)

            def collect(c):
                dve.wait_ge(tapped_steps, sum(POOL_TAPS[:c + 1]) - c - 1)
                dve.wait_ge(tap_steps, sum(len(own_taps(j)) for j in range(c + 1)))
                V.tensor_tensor(hv[:, c, :], prod[:, c % 2, :], hv[:, c, :], ALU.add).then_inc(late_steps, 1)
                dve.wait_ge(late_steps, sum(LATE_TAPS[:c + 1]) + c + 1)
                dve.wait_ge(conv_done, c + 1)
                V.tensor_tensor(hv[:, c, :], bank[6 + c % 2][:], hv[:, c, :], ALU.add).then_inc(hv_ready, 1)

            for c in range(C):
                b = c % 2
                if c == 0:
                    split_lo(p.unit, 0, AHEAD)
                    dve.wait_ge(norm_done, ND["ain"] + 2)
                    V.tensor_scalar(rinv[:], norm[0][:], EPS, None, ALU.mult).then_inc(rinv_ready, 1)
                    dve.wait_ge(rinv_ready, 5)
                    V.tensor_tensor(rinv[:], norm[1][:], rinv[:], ALU.add).then_inc(rinv_ready, 1)
                    V.memset(ssum[:], 0.0).then_inc(ssum_ready, 1)
                    dve.wait_ge(rms_ready, RR["ain"] + 1)
                    V.reciprocal(rinv[:], rms[:]).then_inc(rinv_ready, 1)
                    dve.wait_ge(rinv_ready, 7)
                for j in range(2):
                    k = 2 * b + j
                    dve.wait_ge(chain_done, p.chain + 2 * c + j + 1)
                    V.tensor_tensor(tmp[:, k, :], acc[k][:], rinv[:], ALU.mult).then_inc(acc_free, 1)
                if c == 0:
                    dve.wait_ge(rms_ready, RR["ain"] + 2)
                    V.reciprocal(r1[:], r1[:]).then_inc(rinv_ready, 1)
                else:
                    split_lo(p.unit, 0, 2 * c + AHEAD)
                dve.wait_ge(sig_ready, c + 1)
                if c >= 2:
                    dve.wait_ge(tapped_ready, sum(POOL_TAPS[:c - 1]))
                V.scalar_tensor_tensor(hc[:, b, TAPS - 1:TAPS - 1 + T], tmp[:, 2 * b, :], v("b_in", c),
                                       gate[:, b, :], op0=ALU.add, op1=ALU.mult).then_inc(hc_ready, 1)
                split_lo(p.unit, 0, 2 * c + 1 + AHEAD)
                dve.wait_ge(hc_ready, c + 2)
                dve.wait_ge(hch_ready, c + 1)
                V.tensor_tensor(hcl[:, b, :], hc[:, b, :], hch[:, b, :].bitcast(F32), ALU.subtract)\
                    .then_inc(hcl_ready, 1)
                own, late = own_taps(c), late_taps(c - 1) if c else []
                for n in range(max(len(own), len(late) + LATE_START)):
                    if n < len(own):
                        own_tap(c, n, own[n])
                    if 0 <= n - LATE_START < len(late):
                        late_tap(c - 1, n - LATE_START, late[n - LATE_START])
                if c:
                    collect(c - 1)
            collect(C - 1)
            dve.wait_ge(mean_done, 1)
            for c in range(C):
                V.scalar_tensor_tensor(hv[:, c, :], norm[0][:], -1.0 / D, hv[:, c, :],
                                       op0=ALU.mult, op1=ALU.add).then_inc(xc_ready, 1)
            dve.wait_ge(rms_ready, RR["mlp"])
            V.reciprocal(rinv[:], rms[:]).then_inc(rinv_ready, 1)
            dve.wait_ge(rinv_ready, 9)
            for c in range(C):
                V.tensor_tensor(hv[:, c, :], hv[:, c, :], rinv[:], ALU.mult).then_inc(ln_scaled, 1)
                if c >= 2:
                    dve.wait_ge(ln_hi, c - 1)
                    V.tensor_tensor(ylo[:, c - 2, :], hv[:, c - 2, :], yhi[:, c - 2, :].bitcast(F32),
                                    ALU.subtract).then_inc(ln_lo, 1)
            for c in (C - 2, C - 1):
                dve.wait_ge(ln_hi, c + 1)
                V.tensor_tensor(ylo[:, c, :], hv[:, c, :], yhi[:, c, :].bitcast(F32), ALU.subtract)\
                    .then_inc(ln_lo, 1)
            finish("aout", "mlp", out_bias="b_out")

            feed_forward("mlp", MLP_PARTS, None, None, 10)


def _units(w):
    k, n = w.shape
    return np.ascontiguousarray(w.reshape(k // P, P, n // P, P).transpose(2, 1, 0, 3).reshape(n // P, P, k))


def _cols(v_):
    return v_.reshape(-1, P).T


def kernel(**inputs):
    import concourse.bacc as _bacc
    from concourse.bass_utils import run_bass_kernel_spmd as _run

    a = {k: np.asarray(t) for k, t in inputs.items()}
    w = {}
    w["pool"] = np.ascontiguousarray(
        a["pool_w"][0].reshape(4, 2, P, 2, P).transpose(0, 2, 3, 1, 4).reshape(4, P, 4 * P))
    for layer in range(2):
        wi = a["ffn_w_in"][layer].reshape(D, 2, FF_PAIRS, P).transpose(0, 2, 1, 3).reshape(D, -1)
        at = 0
        for q, n in enumerate(FF_PARTS):
            w[f"ffn{layer}_up{q}"] = _units(wi[:, 2 * at * P:2 * (at + n) * P])
            w[f"ffn{layer}_down{q}"] = _units(a["ffn_w_out"][layer][at * P:(at + n) * P])
            at += n
    heads = [8 * pr + REP * half + i for pr in range(2) for i in range(REP) for half in range(2)]
    nq = HEADS * HD

    def by_head(t):
        return t.reshape(t.shape[:-1] + (HEADS, HD))[..., heads, :].reshape(t.shape)

    wqkv, bqkv = a["attn_w_qkv"][0], a["attn_b_qkv"][0]
    w["qkv"] = _units(np.concatenate([by_head(wqkv[:, :nq]), wqkv[:, nq:]], axis=1))
    bq = np.concatenate([by_head(bqkv[:nq]), bqkv[nq:]])
    w["wo"] = _units(a["attn_w_o"][0])
    w["ain"] = _units(a["a_w_in_2"][0].reshape(D, 2, C, P).transpose(0, 2, 1, 3).reshape(D, -1))
    w["aout"] = _units(a["a_w_out_2"][0])
    at = 0
    for q, n in enumerate(MLP_PARTS):
        w[f"mlp_up{q}"] = _units(a["mlp_w1_2"][0][:, at * P:(at + n) * P])
        w[f"mlp_down{q}"] = _units(a["mlp_w2_2"][0][at * P:(at + n) * P])
        at += n

    glu = np.stack([*a["ffn_conv_w"].transpose(1, 0, 2), a["ffn_conv_b"]], axis=1)
    glu = glu.reshape(2, 4, 2, FF_PAIRS, P).transpose(4, 0, 3, 2, 1).reshape(P, -1)
    parts = {
        "pool_b": _cols(a["pool_b"][0].reshape(-1)), "pool_scale": _cols(a["pool_scale"][0]),
        "g_mix0": _cols(a["norm_mix"][0]), "g_mix1": _cols(a["norm_mix"][1]),
        "g_ffn0": _cols(a["norm_ffn"][0]), "g_ffn1": _cols(a["norm_ffn"][1]),
        "g_final": _cols(a["norm_f"]), "g_mix2": _cols(a["mix_norm_2"][0]), "g_mlp2": _cols(a["mlp_norm_2"][0]),
        "b_qkv": _cols(bq), "b_in": _cols(a["a_b_in_2"][0]), "conv_b": _cols(a["a_conv_b_2"][0]),
        "ln_g": _cols(a["a_ln_g_2"][0]), "ln_b": _cols(a["a_ln_b_2"][0]), "b_out": _cols(a["a_b_out_2"][0]),
        "sinks": np.broadcast_to(a["attn_sinks"][0], (P, HEADS)), "glu": glu,
        "conv_w": a["a_conv_w_2"][0].reshape(TAPS, C, P).transpose(2, 1, 0).reshape(P, -1),
    }
    vec = np.ascontiguousarray(np.concatenate([parts[name] for name, _ in VEC_PARTS], axis=1))

    dist = np.arange(P)[:, None] + P - np.arange(2 * P)[None, :]
    near = np.where((dist >= 0) & (dist < P), -dist, MASKED).astype(np.float32)
    inv = np.broadcast_to((1.0 / np.arange(1, PAD + 1)).astype(np.float32), (P, PAD))
    cst = np.ascontiguousarray(np.concatenate([near, inv, np.eye(P, dtype=np.float32)], axis=1))

    arrays = {"xT": np.ascontiguousarray(a["x"][0].T.reshape(C, P, T).transpose(1, 0, 2)), "vec_in": vec, "cst_in": cst}
    arrays.update({f"w_{k}": t for k, t in w.items()})
    nc = _bacc.Bacc("TRN2", target_bir_lowering=False, num_devices=1)
    aps = {k: nc.dram_tensor(k, t.shape, F32, kind="ExternalInput").ap() for k, t in arrays.items()}
    out = nc.dram_tensor("outT", (P, C, T), F32, kind="ExternalOutput").ap()
    build(nc, aps["xT"], aps["vec_in"], aps["cst_in"], {k: aps[f"w_{k}"] for k in w}, out)
    r = _run(nc, [arrays], core_ids=[0])
    y = r.results[0]["outT"]
    return np.ascontiguousarray(y.transpose(1, 0, 2).reshape(D, T).T)[None]
```

```python
from contextlib import ExitStack

import numpy as np

import concourse.bass as bass
from concourse import mybir

F32 = mybir.dt.float32
F32R = mybir.dt.float32r
ALU = mybir.AluOpType
ACT = mybir.ActivationFunctionType
AX_X = mybir.AxisListType.X

P = 128
D = 1024
T = 512
C = D // P
NBLK = T // P
EPS = 1e-6
WINDOWS = (2, 4, 8, 16)
PAD = max(WINDOWS)
HEADS, KV, HD = 16, 4, 64
REP = HEADS // KV
FF_PAIRS = 2816 // P
FF_PARTS = (8, 8, 6)
MLP_PARTS = (8, 8, 8, 8)
TAPS = 31
PE_TAPS = (9, 8, 7, 7, 7, 7, 12, 13)
POOL_TAPS = (11, 11, 11, 11, 11, 11, 10, 5)
LATE_TAPS = (4, 5, 6, 6, 6, 6, 1, 0)
PARTS = 6
SLOTS = 4
AHEAD = 3
KT = 8
MASKED = -1.0e30

VEC_PARTS = [("pool_b", C), ("pool_scale", C), ("g_mix0", C), ("g_mix1", C), ("g_ffn0", C), ("g_ffn1", C),
             ("g_final", C), ("g_mix2", C), ("g_mlp2", C), ("b_qkv", 12), ("b_in", 2 * C), ("conv_b", C),
             ("ln_g", C), ("ln_b", C), ("b_out", C), ("sinks", HEADS), ("glu", 2 * FF_PAIRS * 8),
             ("conv_w", C * TAPS)]
VEC = {}
_at = 0
for _name, _n in VEC_PARTS:
    VEC[_name] = _at
    _at += _n
VEC_COLS = _at
CST_DIST, CST_INV, CST_ID = 0, 2 * P, 2 * P + PAD
CST_COLS = CST_ID + P


class Phase:

    def __init__(self, name, weights, units, tiles, unit, chain):
        self.name, self.weights, self.units, self.tiles = name, weights, units, tiles
        self.unit, self.chain = unit, chain
        self.end_chain = chain + (2 * units if name == "pool" else units)


def plan(w):
    phases, unit, chain = {}, 0, 0

    def add(name, weights, units, tiles):
        nonlocal unit, chain
        phases[name] = ph = Phase(name, weights, units, tiles, unit, chain)
        unit, chain = unit + units, ph.end_chain

    def add_mlp(kind, parts, per_part):
        order = [("up", 0)]
        for q in range(1, len(parts)):
            order += [("up", q), ("down", q - 1)]
        order.append(("down", len(parts) - 1))
        for what, q in order:
            if what == "up":
                add(f"{kind}_up{q}", w[f"{kind}_up{q}"], per_part * parts[q], C)
            else:
                add(f"{kind}_down{q}", w[f"{kind}_down{q}"], C, parts[q])

    add("pool", w["pool"], 4, 4)
    add_mlp("ffn0", FF_PARTS, 2)
    add("qkv", w["qkv"], 12, C)
    add("wo", w["wo"], C, C)
    add_mlp("ffn1", FF_PARTS, 2)
    add("ain", w["ain"], 2 * C, C)
    add("aout", w["aout"], C, C)
    add_mlp("mlp", MLP_PARTS, 1)
    return phases, unit, chain


def row(t, c):
    if isinstance(c, int):
        return t[:, c, :]
    return t[:, bass.ds(c, 1), :].rearrange("p o n -> p (o n)")


def col(t, e):
    return t[:, e:e + 1] if isinstance(e, int) else t[:, bass.ds(e, 1)]


def run(eng, step, n, peel_first=False, peel_last=False):
    lo, hi = int(peel_first), n - int(peel_last)
    if peel_first:
        step(0)
    if hi - lo == 1:
        step(lo)
    elif hi > lo:
        with eng.Fori(lo, hi) as i:
            step(i)
    if peel_last:
        step(n - 1)


def build(nc, xT, vec_in, cst_in, w_in, out):
    ph, UNITS, CHAINS = plan(w_in)
    order = list(ph.values())

    with ExitStack() as ctx:
        def sb(name, shape, dt=F32, scope=ctx):
            return scope.enter_context(nc.sbuf_tensor(name, shape, dt))

        def sem(name):
            return ctx.enter_context(nc.semaphore(name))

        res = sb("res", [P, C, T])
        with ExitStack() as own:
            bias = sb("bias", [P, HEADS, 2 * P], F32, own)
        xh = sb("xh", [P, C, T], F32R)
        xl = sb("xl", [P, C, T], F32R)
        raw = sb("raw", [P, SLOTS, KT * P])
        whi = sb("whi", [P, SLOTS, KT * P], F32R)
        wlo = sb("wlo", [P, SLOTS, KT * P], F32R)
        vec = sb("vec", [P, VEC_COLS])
        cst = sb("cst", [P, CST_COLS])
        ones = sb("ones", [P, P])
        eps = sb("eps", [P, 2])
        unused = sb("unused", [P, 3])
        gfm = sb("gfm", [P, C])
        pbs = sb("pbs", [P, C])
        r1 = sb("r1", [P, T])
        rms = sb("rms", [P, T])
        rinv = sb("rinv", [P, T])
        ssum = sb("ssum", [P, 2, T])
        sq = sb("sq", [P, 2, T])
        u = sb("u", [P, 4, 2 + T])
        tmp = sb("tmp", [P, 4, T])
        gate = sb("gate", [P, 2, T])
        prod = sb("prod", [P, 2, T])
        with ExitStack() as own:
            ahi = sb("ahi", [P, 2, 8, T], F32R, own)
            alo = sb("alo", [P, 2, 8, T], F32R, own)
        with ExitStack() as own:
            zp = sb("zp", [P, 12, 2, PAD + T], F32, own)
        with ExitStack() as own:
            ohi = sb("ohi", [P, C, T], F32R, own)
        with ExitStack() as own:
            qkvT = sb("qkvT", [P, 12, T], F32, own)
            olo = sb("olo", [P, C, T], F32R, own)
            vt = sb("vt", [P, NBLK, 2, P], F32, own)
            prob = sb("prob", [P, 3, REP, 2 * P], F32, own)
            pT = sb("pT", [P, 2, 2, REP * P], F32, own)
            oq = sb("oq", [P, 2, REP * HD], F32, own)
            stat = sb("stat", [P, 6, NBLK * KV, REP], F32, own)
        with ExitStack() as own:
            ylo = sb("ylo", [P, C, T], F32R, own)
            yhi = sb("yhi", [P, C, T], F32R, own)
        with ExitStack() as own:
            hv = sb("hv", [P, C, T], F32, own)
            hc = sb("hc", [P, 2, TAPS - 1 + T], F32, own)
            hch = sb("hch", [P, 2, TAPS - 1 + T], F32R, own)
            hcl = sb("hcl", [P, 2, TAPS - 1 + T], F32R, own)
            dgh = sb("dgh", [P, 2, max(PE_TAPS) * P], F32R, own)
            dgl = sb("dgl", [P, 2, max(PE_TAPS) * P], F32R, own)
            cwh = sb("cwh", [P, C * TAPS], F32R, own)
            cwl = sb("cwl", [P, C * TAPS], F32, own)
            tapped = sb("tapped", [P, PARTS, T], F32, own)
        bank = [ctx.enter_context(nc.psum_tensor(f"bank{b}", [P, T], F32)) for b in range(8)]
        acc = bank[0:4]
        norm = bank[4:6]
        taps = bank[5]

        x_in = [sem(f"x_in{q}") for q in range(4)]
        head_loaded = sem("head_loaded")
        vec_loaded = sem("vec_loaded")
        cst_loaded = sem("cst_loaded")
        w_loaded = [sem(f"w_loaded{s}") for s in range(SLOTS)]
        hi_done = sem("hi_done")
        lo_done = sem("lo_done")
        chain_done = sem("chain_done")
        acc_free = sem("acc_free")
        setup = sem("setup")
        xh_ready = sem("xh_ready")
        xl_ready = sem("xl_ready")
        sq_ready = sem("sq_ready")
        sq_odd = sem("sq_odd")
        ssum_ready = sem("ssum_ready")
        norm_done = sem("norm_done")
        rms_ready = sem("rms_ready")
        rinv_ready = sem("rinv_ready")
        slide = sem("slide")
        pool_slide = sem("pool_slide")
        res_biased = sem("res_biased")
        pooled = sem("pooled")
        tap2_done = sem("tap2_done")
        tap1_done = sem("tap1_done")
        tap0_done = sem("tap0_done")
        gate_ready = sem("gate_ready")
        prod_ready = sem("prod_ready")
        act_hi = sem("act_hi")
        act_lo = sem("act_lo")
        qkv_ready = sem("qkv_ready")
        vT_done = sem("vT_done")
        v_ready = sem("v_ready")
        scores_done = sem("scores_done")
        bias_ready = sem("bias_ready")
        biased = sem("biased")
        max_steps = sem("max_steps")
        exp_done = sem("exp_done")
        den_steps = sem("den_steps")
        pT_done = sem("pT_done")
        pT_ready = sem("pT_ready")
        pv_done = sem("pv_done")
        o_scaled = sem("o_scaled")
        oT_done = sem("oT_done")
        o_hi = sem("o_hi")
        o_lo = sem("o_lo")
        x2_ready = sem("x2_ready")
        sig_ready = sem("sig_ready")
        hc_ready = sem("hc_ready")
        hch_ready = sem("hch_ready")
        hcl_ready = sem("hcl_ready")
        taps_split = sem("taps_split")
        diag_ready = sem("diag_ready")
        conv_done = sem("conv_done")
        tapped_ready = sem("tapped_ready")
        tapped_steps = sem("tapped_steps")
        tap_steps = sem("tap_steps")
        late_steps = sem("late_steps")
        hv_ready = sem("hv_ready")
        mean_done = sem("mean_done")
        xc_ready = sem("xc_ready")
        xcsq_ready = sem("xcsq_ready")
        early_pair = sem("early_pair")
        late_sums = sem("late_sums")
        sqsum_done = sem("sqsum_done")
        ln_scaled = sem("ln_scaled")
        ln_silu = sem("ln_silu")
        ln_hi = sem("ln_hi")
        ln_lo = sem("ln_lo")
        stored = sem("stored")

        ident = cst[:, CST_ID:CST_ID + P]

        def v(name, e=0):
            return col(vec, VEC[name] + e)

        def bias_of(h):
            return gate[:, h // 2, (h % 2) * 2 * P:(h % 2 + 1) * 2 * P] if h < REP else bias[:, h, :]

        def square_of(c):
            return sq[:, c] if c < 2 else tmp[:, c - 2] if c < 6 else gate[:, c - 6]

        tok = slice(PAD, PAD + T)

        def doublings(g):
            pair = 4 + 2 * g
            steps, src, shift, dst = [], g, 1, pair
            while shift < WINDOWS[g]:
                steps.append((src, dst, shift))
                src, shift, dst = dst, 2 * shift, 2 * pair + 1 - dst
            return steps

        NORMS = ["pool", "ffn0", "qkv", "ffn1", "ain", "mlp"]
        GAIN = {"pool": "g_mix0", "ffn0": "g_ffn0", "qkv": "g_mix1", "ffn1": "g_ffn1", "mlp": "g_mlp2"}
        X = {name: C * k for k, name in enumerate(NORMS)}
        SS = {"qkv": 1, "ffn1": 10, "ain": 19, "mlp": 19 + 17}
        SQ = {"ffn0": 4, "qkv": 12, "ffn1": 20, "ain": 28, "mlp": 44}
        ND = {"qkv": 0, "ffn1": 1, "ain": 2, "mlp": 4}
        RR = {"pool": 0, "ffn0": 1, "qkv": 2, "ffn1": 3, "ain": 4, "mlp": 7}

        pair0, act0 = {}, {}
        pairs = acts = 0
        for name in ph:
            kind, _, part = name.rpartition("_up")
            if kind.startswith("ffn"):
                pair0[name], act0[name] = pairs, acts
                pairs, acts = pairs + FF_PARTS[int(part)], acts + FF_PARTS[int(part)]
            elif kind == "mlp":
                act0[name] = acts
                acts += MLP_PARTS[int(part)]

        def used(unit):
            return 2 * unit + 2 if isinstance(unit, int) and unit < 4 else unit + 5

        def loads(base, i, k):
            return 16 * (i + (base + k) // SLOTS + 1)

        block = ctx.enter_context(nc.Block())

        @block.sync
        def _(sp):
            def load(p, i, k):
                unit = p.unit + SLOTS * i + k
                if isinstance(unit, int) and unit < SLOTS:
                    free, at = None, unit - p.unit
                elif isinstance(i, int):
                    free, at = unit - SLOTS + 1, SLOTS * i + k
                else:
                    free, at = sp.snap(unit - SLOTS + 1), sp.snap(SLOTS * i + k)
                if free is None and k:
                    sp.wait_ge(x_in[k], 16)
                src = p.weights[at] if isinstance(at, int) else \
                    p.weights[bass.ds(at, 1)].rearrange("o p n -> p (o n)")
                if free is not None:
                    sp.wait_ge(lo_done, free)
                sp.dma_start(raw[:, k, 0:p.tiles * P], src).then_inc(w_loaded[k], 16)

            for p in order:
                run(sp, lambda i: [load(p, i, k) for k in range(SLOTS)], p.units // SLOTS)
            last = ph["mlp_down3"]
            for c in range(C):
                sp.wait_ge(acc_free, last.chain + c + 1)
                sp.dma_start(out[:, c, :], res[:, c, :]).then_inc(stored, 16)
            sp.wait_ge(stored, 16 * C)

        @block.gpsimd
        def _(pool):
            for c in range(0, C, 2):
                pool.wait_ge(x_in[c // 2], 16)
                if c >= 2:
                    pool.wait_ge(sqsum_done, c - 1)
                nc.gpsimd.tensor_tensor(sq[:, 0, :], res[:, c, :], res[:, c, :], ALU.mult)\
                    .then_inc(sq_ready, 1)
            pool.wait_ge(setup, 1)
            steps = 0
            for g in (1, 2, 3):
                pool.wait_ge(acc_free, 2 * g + 2)
                for step, (src, dst, shift) in enumerate(doublings(g)):
                    if step:
                        pool.wait_ge(pool_slide, steps)
                    nc.gpsimd.tensor_tensor(zp[:, dst, :, tok], zp[:, src, :, tok],
                                            zp[:, src, :, PAD - shift:PAD - shift + T], ALU.add)\
                        .then_inc(pool_slide, 1)
                    steps += 1

            def add_squares(name):
                per = 2 if name == "ain" else 1
                for n in range(per * C):
                    which, buf = (n % 2, n % 2) if name == "ain" else (0, n % 2)
                    pool.wait_ge(sq_ready, SQ[name] + n + 1)
                    pool.wait_ge(ssum_ready, SS[name] + n + 1)
                    nc.gpsimd.tensor_tensor(ssum[:, which, :], ssum[:, which, :], sq[:, buf, :], ALU.add)\
                        .then_inc(ssum_ready, 1)

            add_squares("qkv")
            pool.wait_ge(cst_loaded, 16)
            pool.wait_ge(prod_ready, FF_PAIRS)
            for h in range(HEADS):
                if h == REP:
                    pool.wait_ge(chain_done, ph["qkv"].end_chain)
                slope = float(np.float32(2.0 ** (-8.0 / HEADS * (h + 1))))
                nc.gpsimd.tensor_scalar(bias_of(h), cst[:, CST_DIST:CST_DIST + 2 * P], slope * HD ** 0.5,
                                        None, ALU.mult).then_inc(bias_ready, 1)
            add_squares("ffn1")
            add_squares("ain")
            made = adds = 0
            for c in range(C):
                if c >= 2:
                    pool.wait_ge(hv_ready, c - 1)
                for k in range(1, POOL_TAPS[c]):
                    a = tapped[:, made % PARTS, :] if k == 1 else prod[:, c % 2, :]
                    pool.wait_ge(tapped_ready, made + k + 1)
                    if k > 1:
                        pool.wait_ge(tapped_steps, adds)
                    nc.gpsimd.tensor_tensor(prod[:, c % 2, :], a, tapped[:, (made + k) % PARTS, :], ALU.add)\
                        .then_inc(tapped_steps, 1)
                    adds += 1
                made += POOL_TAPS[c]
            pool.wait_ge(xcsq_ready, 4)
            nc.gpsimd.tensor_tensor(square_of(2), square_of(2), square_of(3), ALU.add).then_inc(early_pair, 1)
            add_squares("mlp")

        @block.tensor
        def _(pe):
            def three(out_, hi, lo, mh, ml, first, last):
                nc.tensor.matmul(out_, hi, mh, start=first, stop=False)
                nc.tensor.matmul(out_, hi, ml, start=False, stop=False)
                return nc.tensor.matmul(out_, lo, mh, start=False, stop=last)

            def chain(p, i, k, hi, lo):
                chain_no = p.chain + SLOTS * i + k
                pe.wait_ge(lo_done, p.unit + SLOTS * i + k + 1)
                pe.wait_ge(acc_free, chain_no - 3)
                for t in range(p.tiles):
                    w = slice(t * P, (t + 1) * P)
                    mm = three(acc[k][:], whi[:, k, w], wlo[:, k, w], hi[:, t, :], lo[:, t, :],
                               t == 0, t == p.tiles - 1)
                mm.then_inc(chain_done, 1)

            def first_chains(name, norm_name, n=2):
                p = ph[name]
                if norm_name == "ffn0":
                    pe.wait_ge(rms_ready, 1)
                    for c in range(C // 2):
                        sum_square(SQ["ffn0"], c)
                pe.wait_ge(lo_done, p.unit + n)
                pe.wait_ge(acc_free, p.chain + n - 4)
                for t in range(C):
                    if norm_name == "ffn0":
                        if t in (4, 6):
                            sum_square(SQ["ffn0"], t)
                            sum_square(SQ["ffn0"], t + 1)
                    elif t == C - 2:
                        sum_features(norm_name)
                        if norm_name == "ain":
                            sum_features(norm_name, 1)
                    pe.wait_ge(xl_ready, X[norm_name] + t + 1)
                    w = slice(t * P, (t + 1) * P)
                    for k in range(n):
                        mm = three(acc[k][:], whi[:, k, w], wlo[:, k, w], xh[:, t, :], xl[:, t, :],
                                   t == 0, t == C - 1)
                        if t == C - 1:
                            mm.then_inc(chain_done, 1)

            def sum_features(name, which=0):
                adds = 17 if name == "ain" else 9
                pe.wait_ge(ssum_ready, SS[name] + adds)
                if which == 0:
                    pe.wait_ge(rms_ready, RR[name])
                nc.tensor.matmul(norm[which][:], ones[:], ssum[:, which, :], start=True, stop=True)\
                    .then_inc(norm_done, 1)

            def sum_square(count, c):
                pe.wait_ge(sq_ready, count + c + 1)
                mm = nc.tensor.matmul(norm[0][:], ones[:], sq[:, c % 2, :], start=(c == 0), stop=(c == C - 1))
                mm.then_inc(sqsum_done, 1)

            def project(name, first, peel_last=False):
                p = ph[name]

                def step(i):
                    peeled = first is not None and isinstance(i, int) and i == 0
                    n = 2 if peeled else 0
                    if peeled:
                        first_chains(name, first, n)
                    for k in range(n, SLOTS):
                        chain(p, i, k, xh, xl)
                run(pe, step, p.units // SLOTS - int(peel_last), peel_first=first is not None)

            def down(name, buf, acts_before):
                p = ph[name]
                pe.wait_ge(act_lo, acts_before + p.tiles)
                run(pe, lambda i: [chain(p, i, k, ahi[:, buf], alo[:, buf]) for k in range(SLOTS)],
                    C // SLOTS)

            def feed_forward(kind, parts):
                for q in range(len(parts)):
                    project(f"{kind}_up{q}", kind if q == 0 else None)
                    if q:
                        down(f"{kind}_down{q - 1}", (q - 1) % 2, act0[f"{kind}_up{q - 1}"])
                q = len(parts) - 1
                down(f"{kind}_down{q}", q % 2, act0[f"{kind}_up{q}"])

            pe.wait_ge(setup, 1)
            for c in range(C):
                if c % 2:
                    pe.wait_ge(sq_odd, c // 2 + 1)
                else:
                    pe.wait_ge(sq_ready, c // 2 + 1)
                nc.tensor.matmul(norm[0][:], ones[:], sq[:, c % 2, :], start=(c == 0), stop=(c == C - 1))\
                    .then_inc(sqsum_done, 1)
            for g in range(4):
                pe.wait_ge(lo_done, g + 1)
                for o in range(2):
                    c = 2 * g + o
                    if c >= 4:
                        pe.wait_ge(acc_free, c - 3)
                    for t in range(2):
                        pe.wait_ge(xl_ready, 2 * g + t + 1)
                        w = slice((2 * o + t) * P, (2 * o + t + 1) * P)
                        mm = three(acc[c % 4][:], whi[:, g, w], wlo[:, g, w], xh[:, 2 * g + t, :],
                                   xl[:, 2 * g + t, :], t == 0, t == 1)
                    mm.then_inc(chain_done, 1)
            feed_forward("ffn0", FF_PARTS)

            p = ph["qkv"]
            project("qkv", "qkv", peel_last=True)
            for k in range(SLOTS - 1):
                chain(p, 2, k, xh, xl)
            STEPS = [(n, g) for n in range(NBLK) for g in range(KV)]

            def keys(n):
                return P if n == 0 else 0

            def scores(s):
                n, g = STEPS[s]
                k0, half = keys(n), slice(HD * (g % 2), HD * (g % 2) + HD)
                if s >= 2:
                    pe.wait_ge(biased, REP * (s - 1))
                for i in range(REP):
                    o = (i % 2) * 2 * P
                    mm = nc.tensor.matmul(acc[2 * (s % 2) + i // 2][:, o + k0:o + 2 * P],
                                          qkvT[half, 4 * (g // 2) + i, n * P:(n + 1) * P],
                                          qkvT[half, 8 + g // 2, (n - 1) * P + k0:(n + 1) * P],
                                          start=True, stop=True)
                mm.then_inc(scores_done, 1)

            def transposes(s):
                n, _ = STEPS[s]
                pe.wait_ge(exp_done, s + 1)
                if s >= 1:
                    pe.wait_ge(pT_ready, s)
                for b in range(keys(n) // P, 2):
                    for i in range(REP):
                        mm = nc.tensor.transpose(bank[4 + b][:, i * P:(i + 1) * P],
                                                 prob[:, s % 3, i, b * P:(b + 1) * P], ident)
                mm.then_inc(pT_done, 1)

            def values(s):
                n, g = STEPS[s]
                pe.wait_ge(pT_ready, s + 1)
                if s == 0:
                    pe.wait_ge(v_ready, 2)
                else:
                    pe.wait_ge(o_scaled, s)
                half = slice(HD * (g % 2), HD * (g % 2) + HD)
                b0 = keys(n) // P
                for i in range(REP):
                    for b in range(b0, 2):
                        mm = nc.tensor.matmul(bank[6][:, i * HD:(i + 1) * HD], pT[:, s % 2, b, i * P:(i + 1) * P],
                                              vt[:, n - 1 + b, g // 2, half], start=(b == b0), stop=(b == 1))
                mm.then_inc(pv_done, 1)

            def out_transposes(s):
                pe.wait_ge(o_scaled, s + 1)
                if s == 0:
                    pe.wait_ge(v_ready, 2)
                else:
                    pe.wait_ge(o_lo, s)
                for j in range(2):
                    mm = nc.tensor.transpose(bank[7][:, j * P:(j + 1) * P], oq[:, s % 2, j * P:(j + 1) * P], ident)
                mm.then_inc(oT_done, 1)

            last = len(STEPS) - 1
            pe.wait_ge(cst_loaded, 16)
            pe.wait_ge(qkv_ready, 10)
            scores(0)
            chain(p, 2, SLOTS - 1, xh, xl)
            pe.wait_ge(qkv_ready, 12)
            scores(1)
            for pr in range(2):
                for n in range(NBLK):
                    mm = nc.tensor.transpose(bank[6 + pr][:, n * P:(n + 1) * P],
                                             qkvT[:, 10 + pr, n * P:(n + 1) * P], ident)
                mm.then_inc(vT_done, 1)
            p = ph["wo"]

            def wo_tiles(chunks):
                for t in chunks:
                    pe.wait_ge(o_lo, last - 2 + t // 2)
                    w = slice(t * P, (t + 1) * P)
                    for k in range(2):
                        mm = three(acc[k][:], whi[:, k, w], wlo[:, k, w], ohi[:, t, :], olo[:, t, :],
                                   t == 0, t == C - 1)
                        if t == C - 1:
                            mm.then_inc(chain_done, 1)

            for s in range(last + 3):
                if s + 2 <= last:
                    scores(s + 2)
                if s <= last:
                    transposes(s)
                if s == last:
                    pe.wait_ge(lo_done, p.unit + 2)
                    pe.wait_ge(biased, REP * last)
                    wo_tiles((0, 1))
                if 1 <= s <= last + 1:
                    values(s - 1)
                if s >= 2:
                    out_transposes(s - 2)
                if s == last + 1:
                    wo_tiles((2, 3))

            wo_tiles((4, 5, 6, 7))
            pe.wait_ge(biased, REP * len(STEPS))
            for k in range(2, p.units):
                chain(p, k // SLOTS, k % SLOTS, ohi, olo)

            feed_forward("ffn1", FF_PARTS)

            p = ph["ain"]

            def convolve(c):
                b = c % 2
                pe.wait_ge(hcl_ready, c + 1)
                pe.wait_ge(diag_ready, c + 1)
                if c >= 2:
                    pe.wait_ge(hv_ready, c - 1)
                for k in range(PE_TAPS[c]):
                    w = slice(k * P, (k + 1) * P)
                    mm = three(bank[6 + b][:], dgh[:, b, w], dgl[:, b, w], hch[:, b, k:k + T],
                               hcl[:, b, k:k + T], k == 0, k == PE_TAPS[c] - 1)
                mm.then_inc(conv_done, 1)

            def feature_sum(c):
                if c == 0:
                    pe.wait_ge(rms_ready, RR["ain"] + 2)
                pe.wait_ge(hv_ready, c + 1)
                mm = nc.tensor.matmul(norm[0][:], ones[:], hv[:, c, :], start=(c == 0), stop=(c == C - 1))
                if c == C - 1:
                    mm.then_inc(mean_done, 1)

            for c in range(C):
                if c == 0:
                    first_chains("ain", "ain")
                for k in (2 * (c % 2), 2 * (c % 2) + 1) if c else ():
                    chain(p, c // 2, k, xh, xl)
                if c >= 1:
                    convolve(c - 1)
                if c >= 2:
                    feature_sum(c - 2)
            convolve(C - 1)
            feature_sum(C - 2)
            feature_sum(C - 1)
            for done, count, c in ((xcsq_ready, 1, 0), (xcsq_ready, 2, 1), (early_pair, 1, 2), (late_sums, 3, 4)):
                pe.wait_ge(done, count)
                mm = nc.tensor.matmul(norm[1][:], ones[:], square_of(c), start=(c == 0), stop=(c == 4))
            mm.then_inc(sqsum_done, 1)
            p = ph["aout"]
            pe.wait_ge(lo_done, p.unit + 2)
            pe.wait_ge(acc_free, p.chain - 2)
            for t in range(C):
                pe.wait_ge(ln_lo, t + 1)
                w = slice(t * P, (t + 1) * P)
                for k in range(2):
                    mm = three(acc[k][:], whi[:, k, w], wlo[:, k, w], yhi[:, t, :], ylo[:, t, :],
                               t == 0, t == C - 1)
                    if t == C - 1:
                        mm.then_inc(chain_done, 1)
            for k in range(2, p.units):
                chain(p, k // SLOTS, k % SLOTS, yhi, ylo)

            feed_forward("mlp", MLP_PARTS)

        @block.scalar
        def _(act):
            def split_hi(base, i, k, tiles=KT):
                if isinstance(i, int) and base + SLOTS * i + k >= UNITS:
                    return
                s, unit = k % SLOTS, base + SLOTS * i + k
                act.wait_ge(w_loaded[s], loads(base, i, k))
                if not (isinstance(unit, int) and unit < SLOTS):
                    act.wait_ge(chain_done, used(unit - SLOTS))
                nc.scalar.activation(whi[:, s, 0:tiles * P], raw[:, s, 0:tiles * P], ACT.Copy)\
                    .then_inc(hi_done, 1)

            def prepare(name, c, buf, reads_done):
                if name == "ain":
                    gain = col(gfm, c)
                else:
                    gain = v(GAIN[name], c)
                if name in SS:
                    act.wait_ge(ssum_ready, SS[name] + (1 + 2 * c if name == "ain" else c))
                if reads_done:
                    act.wait_ge(chain_done, reads_done)
                nc.scalar.activation(row(xh, c), row(res, c), ACT.Copy, scale=gain).then_inc(xh_ready, 1)
                if name == "pool":
                    return
                if name == "ain":
                    nc.scalar.activation(sq[:, 0, :], row(res, c), ACT.Square).then_inc(sq_ready, 1)
                    nc.scalar.activation(sq[:, 1, :], row(res, c), ACT.Square, scale=v("g_final", c))\
                        .then_inc(sq_ready, 1)
                else:
                    nc.scalar.activation(sq[:, buf, :], row(res, c), ACT.Square).then_inc(sq_ready, 1)

            def root(name, which=0):
                if name == "ffn0":
                    act.wait_ge(sqsum_done, 2 * C)
                else:
                    act.wait_ge(norm_done, ND[name] + 1)
                nc.scalar.activation(rms[:], norm[which][:], ACT.Sqrt, scale=1.0 / D, bias=eps[:, 0:1])\
                    .then_inc(rms_ready, 1)

            def finish(name, norm_name, reads_done):
                p = ph[name]

                def step(i):
                    for k in range(SLOTS):
                        split_hi(p.unit, i, k + AHEAD)
                        act.wait_ge(acc_free, p.chain + SLOTS * i + k + 1)
                        prepare(norm_name, SLOTS * i + k, k % 2, reads_done)
                run(act, step, C // SLOTS)

            def plain(name, peel_last=False):
                p = ph[name]
                run(act, lambda i: [split_hi(p.unit, i, k + AHEAD) for k in range(SLOTS)], p.units // SLOTS,
                    peel_last=peel_last)

            def ffn_up(name, layer, buf, first, buffer_free):
                p = ph[name]
                pair_base, act_base, q0 = pair0[name], act0[name], pair0[name] % FF_PAIRS

                def step(i):
                    for b in range(2):
                        pair = pair_base + 2 * i + b
                        for j in range(2):
                            k = 2 * b + j
                            split_hi(p.unit, i, k + AHEAD)
                            if first and isinstance(i, int) and i == 0 and k == 0:
                                root(first)
                            par = VEC["glu"] + ((layer * FF_PAIRS + q0) * 2 + k) * 4 + 16 * i
                            act.wait_ge(acc_free, p.chain + SLOTS * i + k + 1)
                            act.wait_ge(vec_loaded, 16)
                            nc.scalar.activation(tmp[:, k, :], u[:, k, 2:2 + T], ACT.Identity,
                                                 scale=col(vec, par + 2), bias=col(vec, par + 3))\
                                .then_inc(tap2_done, 1)
                        act.wait_ge(tap0_done, 2 * pair + 2)
                        nc.scalar.activation(gate[:, b, :], tmp[:, 2 * b + 1, :], ACT.Silu)\
                            .then_inc(gate_ready, 1)
                        act.wait_ge(prod_ready, act_base + 2 * i + b + 1)
                        act.wait_ge(chain_done, buffer_free)
                        nc.scalar.activation(row(ahi[:, buf], 2 * i + b), prod[:, b, :], ACT.Copy)\
                            .then_inc(act_hi, 1)
                run(act, step, p.units // SLOTS, peel_first=bool(first))

            def mlp_up(name, buf, first, buffer_free):
                p, act_base = ph[name], act0[name]

                def step(i):
                    for k in range(SLOTS):
                        split_hi(p.unit, i, k + AHEAD)
                        if first and isinstance(i, int) and i == 0 and k == 0:
                            root(first)
                        act.wait_ge(prod_ready, act_base + SLOTS * i + k + 1)
                        act.wait_ge(chain_done, buffer_free)
                        nc.scalar.activation(row(ahi[:, buf], SLOTS * i + k), tmp[:, k, :], ACT.Copy)\
                            .then_inc(act_hi, 1)
                run(act, step, p.units // SLOTS, peel_first=bool(first))

            def feed_forward(kind, parts, layer, next_norm):
                n = len(parts)
                for q in range(n):
                    up = f"{kind}_up{q}"
                    free = ph[f"{kind}_down{q - 2}"].end_chain if q >= 2 else ph[up].chain
                    if kind == "mlp":
                        mlp_up(up, q % 2, kind if q == 0 else None, free)
                    else:
                        ffn_up(up, layer, q % 2, kind if q == 0 else None, free)
                    if q:
                        plain(f"{kind}_down{q - 1}")
                if next_norm:
                    finish(f"{kind}_down{n - 1}", next_norm, ph[f"{kind}_up{n - 1}"].end_chain)
                else:
                    plain(f"{kind}_down{n - 1}", peel_last=True)

            head = VEC["glu"]
            act.dma_start(vec[:, 0:head], vec_in[:, 0:head]).then_inc(head_loaded, 16)
            for q in range(4):
                act.dma_start(res[:, 2 * q:2 * q + 2, :], xT[:, 2 * q:2 * q + 2, :]).then_inc(x_in[q], 16)
            act.dma_start(vec[:, head:], vec_in[:, head:]).then_inc(vec_loaded, 16)
            act.dma_start(cst[:], cst_in).then_inc(cst_loaded, 16)

            act.wait_ge(setup, 1)
            nc.scalar.activation(unused[:, 0:1], eps[:, 0:1], ACT.Sqrt)
            act.wait_ge(setup, 2)
            act.wait_ge(head_loaded, 16)
            for c in range(C):
                if c % 2 == 0:
                    act.wait_ge(x_in[c // 2], 16)
                if c % 2:
                    if c >= 2:
                        act.wait_ge(sqsum_done, c - 1)
                    nc.scalar.activation(sq[:, 1, :], res[:, c, :], ACT.Square).then_inc(sq_odd, 1)
                prepare("pool", c, c % 2, 0)
                if c in (1, 3, 5, 6):
                    split_hi(0, 0, (1, 3, 5, 6).index(c), 4)
            act.wait_ge(sqsum_done, C)
            nc.scalar.activation(rms[:], norm[0][:], ACT.Sqrt, scale=1.0 / D, bias=eps[:, 0:1])\
                .then_inc(rms_ready, 1)
            for c in range(C):
                act.wait_ge(xl_ready, c + 1)
                nc.scalar.activation(res[:, c, :], res[:, c, :], ACT.Identity, bias=col(pbs, c))\
                    .then_inc(res_biased, 1)
                if c in (1, 3, 5):
                    split_hi(0, 0, 4 + c // 2)
            for c in range(C):
                act.wait_ge(pooled, c + 1)
                if c >= 2:
                    act.wait_ge(sqsum_done, C + c - 1)
                prepare("ffn0", c, c % 2, 2 * (c // 2) + 2)

            feed_forward("ffn0", FF_PARTS, 0, "qkv")

            p = ph["qkv"]

            def qkv_step(i):
                for k in range(SLOTS):
                    split_hi(p.unit, i, k + AHEAD)
                    if isinstance(i, int) and i + k == 0:
                        root("qkv")
                    m = SLOTS * i + k
                    if isinstance(i, int) and m == p.units - 1:
                        exps(0)
                    act.wait_ge(acc_free, p.chain + m + 1)
                    act.wait_ge(vec_loaded, 16)
                    nc.scalar.activation(row(qkvT, m), tmp[:, k, :], ACT.Identity, bias=v("b_qkv", m))\
                        .then_inc(qkv_ready, 1)

            def copy_v(pr):
                act.wait_ge(vT_done, pr + 1)
                nc.scalar.activation(vt[:, :, pr, :], bank[6 + pr][:].rearrange("p (n d) -> p n d", n=NBLK),
                                     ACT.Copy).then_inc(v_ready, 1)

            def exps(s):
                k0 = P if s // KV == 0 else 0
                act.wait_ge(max_steps, 2 * (s + 1))
                for i in range(REP):
                    a = prob[:, s % 3, i, k0:2 * P]
                    nc.scalar.activation(a, a, ACT.Exp, bias=stat[:, 1, s, i:i + 1],
                                         accum_out=stat[:, 3, s, i:i + 1])
                nc.scalar.activation(stat[:, 4, s, :], stat[:, 2, s, :], ACT.Exp).then_inc(exp_done, 1)

            def copy_pT(s):
                b0 = 1 if s // KV == 0 else 0
                act.wait_ge(pT_done, s + 1)
                if s >= 2:
                    act.wait_ge(pv_done, s - 1)
                for b in range(b0, 2):
                    last = nc.scalar.activation(pT[:, s % 2, b, :], bank[4 + b][:], ACT.Copy)
                last.then_inc(pT_ready, 1)

            def out_hi(s):
                n, g = s // KV, s % KV
                act.wait_ge(oT_done, s + 1)
                nc.scalar.activation(ohi[:, 2 * g:2 * g + 2, n * P:(n + 1) * P],
                                     bank[7][:, 0:2 * P].rearrange("p (j q) -> p j q", j=2), ACT.Copy)\
                    .then_inc(o_hi, 1)

            last = NBLK * KV - 1
            run(act, qkv_step, 3, peel_first=True, peel_last=True)
            copy_v(0)
            copy_v(1)
            for s in range(last + 4):
                if s >= 3:
                    out_hi(s - 3)
                if s + 1 <= last:
                    exps(s + 1)
                if s <= last:
                    copy_pT(s)
            finish("wo", "ffn1", ph["qkv"].end_chain)

            feed_forward("ffn1", FF_PARTS, 1, "ain")

            nc.scalar.activation(cwh[:], vec[:, VEC["conv_w"]:VEC["conv_w"] + C * TAPS], ACT.Copy)\
                .then_inc(taps_split, 1)
            p = ph["ain"]

            def diagonals(c):
                if c >= 2:
                    act.wait_ge(conv_done, c - 1)
                for k in range(PE_TAPS[c]):
                    e = c * TAPS + k
                    nc.scalar.activation(dgh[:, c % 2, k * P:(k + 1) * P], ident, ACT.Copy,
                                         scale=cwh[:, e:e + 1].bitcast(F32))
                    last = nc.scalar.activation(dgl[:, c % 2, k * P:(k + 1) * P], ident, ACT.Copy,
                                                scale=cwl[:, e:e + 1])
                last.then_inc(diag_ready, 1)

            def products(c, ks):
                for k in ks:
                    n = sum(POOL_TAPS[:c]) + k
                    if n >= PARTS:
                        m = n - PARTS
                        cm = next(j for j in range(C) if m < sum(POOL_TAPS[:j + 1]))
                        act.wait_ge(tapped_steps, sum(POOL_TAPS[:cm]) - cm + max(m - sum(POOL_TAPS[:cm]), 1))
                    tap = PE_TAPS[c] + k
                    nc.scalar.activation(tapped[:, n % PARTS, :], hc[:, c % 2, tap:tap + T], ACT.Identity,
                                         scale=v("conv_w", c * TAPS + tap),
                                         bias=v("conv_b", c) if k == 0 else 0.0).then_inc(tapped_ready, 1)

            nc.scalar.activation(unused[:, 1:2], eps[:, 0:1], ACT.Sqrt)
            for c in range(C):
                if c < C - 1:
                    split_hi(p.unit, 0, 2 * c + AHEAD)
                if c == 0:
                    act.wait_ge(rinv_ready, 6)
                    nc.scalar.activation(rms[:], rinv[:], ACT.Sqrt, scale=1.0 / D, bias=eps[:, 1:2])\
                        .then_inc(rms_ready, 1)
                    nc.scalar.activation(r1[:], norm[0][:], ACT.Sqrt, scale=1.0 / D, bias=eps[:, 0:1])\
                        .then_inc(rms_ready, 1)
                    act.wait_ge(taps_split, 2)
                    diagonals(0)
                act.wait_ge(acc_free, p.chain + 2 * c + 2)
                nc.scalar.activation(gate[:, c % 2, :], tmp[:, 2 * (c % 2) + 1, :], ACT.Sigmoid,
                                     bias=v("b_in", C + c)).then_inc(sig_ready, 1)
                if c < C - 1:
                    split_hi(p.unit, 0, 2 * c + 1 + AHEAD)
                if 1 <= c < C - 1:
                    products(c - 1, range(PARTS, POOL_TAPS[c - 1]))
                act.wait_ge(hc_ready, c + 2)
                if c >= 2:
                    act.wait_ge(conv_done, c - 1)
                nc.scalar.activation(hch[:, c % 2, :], hc[:, c % 2, :], ACT.Copy).then_inc(hch_ready, 1)
                if c == C - 1:
                    products(c - 1, range(PARTS, POOL_TAPS[c - 1]))
                products(c, range(min(PARTS, POOL_TAPS[c])))
                if c + 1 < C:
                    diagonals(c + 1)
                else:
                    split_hi(p.unit, 0, 2 * c + AHEAD)
                    split_hi(p.unit, 0, 2 * c + 1 + AHEAD)
            products(C - 1, range(PARTS, POOL_TAPS[C - 1]))
            nc.scalar.activation(unused[:, 2:3], eps[:, 0:1], ACT.Sqrt)
            for c in range(C):
                act.wait_ge(xc_ready, c + 1)
                nc.scalar.activation(square_of(c), hv[:, c, :], ACT.Square).then_inc(xcsq_ready, 1)
            act.wait_ge(sqsum_done, 2 * C + 1)
            nc.scalar.activation(rms[:], norm[1][:], ACT.Sqrt, scale=1.0 / D, bias=eps[:, 0:1]).then_inc(rms_ready, 1)
            for c in range(C):
                act.wait_ge(ln_scaled, c + 1)
                nc.scalar.activation(hv[:, c, :], hv[:, c, :], ACT.Silu, scale=v("ln_g", c), bias=v("ln_b", c))\
                    .then_inc(ln_silu, 1)
                act.wait_ge(ln_silu, c + 1)
                nc.scalar.activation(yhi[:, c, :], hv[:, c, :], ACT.Copy).then_inc(ln_hi, 1)
            finish("aout", "mlp", ph["ain"].end_chain)

            feed_forward("mlp", MLP_PARTS, None, None)

        @block.vector
        def _(dve):
            V = nc.vector

            def split_lo(base, i, k, tiles=KT):
                if isinstance(i, int) and base + SLOTS * i + k >= UNITS:
                    return
                s = k % SLOTS
                dve.wait_ge(hi_done, base + SLOTS * i + k + 1)
                V.tensor_tensor(wlo[:, s, 0:tiles * P], raw[:, s, 0:tiles * P],
                                whi[:, s, 0:tiles * P].bitcast(F32), ALU.subtract).then_inc(lo_done, 1)

            def prepare(name, c):
                gain = col(gfm, c) if name == "ain" else v(GAIN[name], c)
                dve.wait_ge(xh_ready, X[name] + c + 1)
                V.scalar_tensor_tensor(row(xl, c), row(res, c), gain, row(xh, c).bitcast(F32),
                                       op0=ALU.mult, op1=ALU.subtract).then_inc(xl_ready, 1)

            def invert(name, k0):
                dve.wait_ge(rms_ready, RR[name] + 1)
                V.reciprocal(rinv[:], rms[:]).then_inc(rinv_ready, 1)
                if name in SS:
                    V.memset(ssum[:], 0.0).then_inc(ssum_ready, 1)
                dve.wait_ge(rinv_ready, k0)

            def add_residual(p, i, k):
                c = SLOTS * i + k
                dve.wait_ge(chain_done, p.chain + c + 1)
                V.tensor_tensor(row(res, c), acc[k][:], row(res, c), ALU.add).then_inc(acc_free, 1)

            def finish(name, norm_name, out_bias=None):
                p = ph[name]

                def step(i):
                    for k in range(SLOTS):
                        c = SLOTS * i + k
                        if out_bias:
                            V.scalar_tensor_tensor(row(res, c), row(res, c), v("g_final", c), r1[:],
                                                   op0=ALU.mult, op1=ALU.mult).then_inc(x2_ready, 1)
                            dve.wait_ge(x2_ready, c + 1)
                            dve.wait_ge(chain_done, p.chain + c + 1)
                            V.scalar_tensor_tensor(row(res, c), acc[k][:], v(out_bias, c), row(res, c),
                                                   op0=ALU.add, op1=ALU.add).then_inc(acc_free, 1)
                        else:
                            add_residual(p, i, k)
                        split_lo(p.unit, i, k + AHEAD)
                        prepare(norm_name, c)
                run(dve, step, C // SLOTS)

            def plain_down(name, peel_last=False):
                p = ph[name]

                def step(i):
                    for k in range(SLOTS):
                        split_lo(p.unit, i, k + AHEAD)
                        add_residual(p, i, k)
                run(dve, step, C // SLOTS, peel_last=peel_last)

            def ffn_up(name, layer, buf, first, rinv_count):
                p = ph[name]
                pair_base, act_base, q0 = pair0[name], act0[name], pair0[name] % FF_PAIRS

                def step(i):
                    for b in range(2):
                        pair = pair_base + 2 * i + b
                        par = VEC["glu"] + ((layer * FF_PAIRS + q0) * 2 + 2 * b) * 4 + 16 * i
                        split_lo(p.unit, i, 2 * b + AHEAD)
                        if first and isinstance(i, int) and i == 0 and b == 0:
                            invert(first, rinv_count)
                        for j in range(2):
                            k = 2 * b + j
                            dve.wait_ge(chain_done, p.chain + SLOTS * i + k + 1)
                            V.tensor_tensor(u[:, k, 2:2 + T], acc[k][:], rinv[:], ALU.mult).then_inc(acc_free, 1)
                        for shift, done, before in ((1, tap1_done, tap2_done), (0, tap0_done, tap1_done)):
                            for j in range(2):
                                k = 2 * b + j
                                dve.wait_ge(before, 2 * pair + j + 1)
                                V.scalar_tensor_tensor(tmp[:, k, :], u[:, k, shift:shift + T],
                                                       col(vec, par + 4 * j + shift), tmp[:, k, :],
                                                       op0=ALU.mult, op1=ALU.add).then_inc(done, 1)
                        split_lo(p.unit, i, 2 * b + 1 + AHEAD)
                        dve.wait_ge(gate_ready, pair + 1)
                        V.tensor_tensor(prod[:, b, :], tmp[:, 2 * b, :], gate[:, b, :], ALU.mult)\
                            .then_inc(prod_ready, 1)
                        dve.wait_ge(act_hi, act_base + 2 * i + b + 1)
                        V.tensor_tensor(row(alo[:, buf], 2 * i + b), prod[:, b, :],
                                        row(ahi[:, buf], 2 * i + b).bitcast(F32), ALU.subtract)\
                            .then_inc(act_lo, 1)
                run(dve, step, p.units // SLOTS, peel_first=bool(first))

            def mlp_up(name, buf, first, rinv_count):
                p, act_base = ph[name], act0[name]

                def step(i):
                    for k in range(SLOTS):
                        split_lo(p.unit, i, k + AHEAD)
                        if first and isinstance(i, int) and i == 0 and k == 0:
                            invert(first, rinv_count)
                        a = act_base + SLOTS * i + k
                        dve.wait_ge(chain_done, p.chain + SLOTS * i + k + 1)
                        V.tensor_tensor(u[:, k, 2:2 + T], acc[k][:], rinv[:], ALU.mult).then_inc(acc_free, 1)
                        dve.wait_ge(acc_free, p.chain + SLOTS * i + k + 1)
                        V.scalar_tensor_tensor(tmp[:, k, :], u[:, k, 2:2 + T], 0.0, u[:, k, 2:2 + T],
                                               op0=ALU.max, op1=ALU.mult).then_inc(prod_ready, 1)
                        dve.wait_ge(act_hi, a + 1)
                        V.tensor_tensor(row(alo[:, buf], SLOTS * i + k), tmp[:, k, :],
                                        row(ahi[:, buf], SLOTS * i + k).bitcast(F32), ALU.subtract)\
                            .then_inc(act_lo, 1)
                run(dve, step, p.units // SLOTS, peel_first=bool(first))

            def feed_forward(kind, parts, layer, next_norm, rinv_count):
                n = len(parts)
                for q in range(n):
                    if kind == "mlp":
                        mlp_up(f"{kind}_up{q}", q % 2, kind if q == 0 else None, rinv_count)
                    else:
                        ffn_up(f"{kind}_up{q}", layer, q % 2, kind if q == 0 else None, rinv_count)
                    if q:
                        plain_down(f"{kind}_down{q - 1}")
                if next_norm:
                    finish(f"{kind}_down{n - 1}", next_norm)
                else:
                    plain_down(f"{kind}_down{n - 1}", peel_last=True)

            V.memset(ones[:], 1.0)
            V.memset(eps[:, 0:1], EPS)
            V.memset(eps[:, 1:2], EPS * EPS)
            V.memset(u[:, :, 0:2], 0.0)
            V.memset(zp[:, :, :, 0:PAD], 0.0).then_inc(setup, 1)
            V.memset(ssum[:, 0, :], 0.0).then_inc(ssum_ready, 1)
            V.memset(ssum[:, 1, :], 0.0).then_inc(ssum_ready, 1)
            dve.wait_ge(head_loaded, 16)
            V.tensor_tensor(pbs[:], vec[:, VEC["pool_b"]:VEC["pool_b"] + C],
                            vec[:, VEC["pool_scale"]:VEC["pool_scale"] + C], ALU.mult)
            V.tensor_tensor(gfm[:], vec[:, VEC["g_final"]:VEC["g_final"] + C],
                            vec[:, VEC["g_mix2"]:VEC["g_mix2"] + C], ALU.mult).then_inc(setup, 1)

            for c in range(C):
                prepare("pool", c)
                if c in (1, 3, 5, 6):
                    split_lo(0, 0, (1, 3, 5, 6).index(c), 4)
            invert("pool", 1)
            steps = 0

            def stepped(ins):
                nonlocal steps
                steps += 1
                ins.then_inc(slide, 1)
                dve.wait_ge(slide, steps)

            def project_out(g):
                for c in (2 * g, 2 * g + 1):
                    dve.wait_ge(chain_done, c + 1)
                    V.tensor_tensor(zp[:, g, c % 2, tok], acc[c % 4][:], rinv[:], ALU.mult).then_inc(acc_free, 1)

            def window_sums(g):
                dve.wait_ge(acc_free, 2 * g + 2)
                for src, dst, shift in doublings(g):
                    stepped(V.tensor_tensor(zp[:, dst, :, tok], zp[:, src, :, tok],
                                            zp[:, src, :, PAD - shift:PAD - shift + T], ALU.add))

            def add_pooled(g):
                win, total = WINDOWS[g], zp[:, doublings(g)[-1][1]]
                z, y = zp[:, g], tmp[:, 2 * (g % 2):2 * (g % 2) + 2, :]
                if g >= 1:
                    dve.wait_ge(pool_slide, sum(len(doublings(j)) for j in range(1, g + 1)))
                e = win - 1
                inv = cst[:, CST_INV:CST_INV + e]
                for o in range(2):
                    V.tensor_tensor(prod[:, o, 0:e], total[:, o, PAD:PAD + e], inv, ALU.mult)
                stepped(V.scalar_tensor_tensor(y, total[:, :, tok], 1.0 / win, z[:, :, tok],
                                               op0=ALU.mult, op1=ALU.subtract))
                stepped(V.tensor_tensor(y[:, :, 0:e], prod[:, :, 0:e], z[:, :, PAD:PAD + e], ALU.subtract))
                for o in range(2):
                    c = 2 * g + o
                    dve.wait_ge(res_biased, c + 1)
                    V.scalar_tensor_tensor(res[:, c, :], y[:, o, :], v("pool_scale", c), res[:, c, :],
                                           op0=ALU.mult, op1=ALU.add).then_inc(pooled, 1)

            project_out(0)
            project_out(1)
            project_out(2)
            project_out(3)
            window_sums(0)
            dve.wait_ge(cst_loaded, 16)
            for g in range(len(WINDOWS)):
                add_pooled(g)
                if g < 2:
                    split_lo(0, 0, 4 + g)
                prepare("ffn0", 2 * g)
                prepare("ffn0", 2 * g + 1)
            split_lo(0, 0, 6)

            feed_forward("ffn0", FF_PARTS, 0, "qkv", 2)

            p = ph["qkv"]

            def qkv_step(i):
                for k in range(SLOTS):
                    split_lo(p.unit, i, k + AHEAD)
                    if isinstance(i, int) and SLOTS * i + k == p.units - 1:
                        front(0)
                    if isinstance(i, int) and i + k == 0:
                        invert("qkv", 3)
                    dve.wait_ge(chain_done, p.chain + SLOTS * i + k + 1)
                    if not (isinstance(i, int) and i == 0):
                        dve.wait_ge(qkv_ready, SLOTS * i + k - 3)
                    V.tensor_tensor(tmp[:, k, :], acc[k][:], rinv[:], ALU.mult).then_inc(acc_free, 1)

            def front(s):
                k0, g = P if s // KV == 0 else 0, s % KV
                dve.wait_ge(scores_done, s + 1)
                dve.wait_ge(bias_ready, REP * (g + 1))
                if s >= 3:
                    dve.wait_ge(pT_done, s - 2)
                for i in range(REP):
                    o, h = (i % 2) * 2 * P, REP * g + i
                    V.tensor_tensor_reduce(out=prob[:, s % 3, i, k0:2 * P],
                                           in0=acc[2 * (s % 2) + i // 2][:, o + k0:o + 2 * P],
                                           in1=bias_of(h)[:, k0:2 * P], scale=HD ** -0.5, scalar=v("sinks", h),
                                           op0=ALU.add, op1=ALU.max, accum_out=stat[:, 0, s, i:i + 1])\
                        .then_inc(biased, 1)
                dve.wait_ge(biased, REP * (s + 1))
                V.tensor_scalar(stat[:, 1, s, :], stat[:, 0, s, :], -1.0, None, ALU.mult).then_inc(max_steps, 1)
                V.tensor_tensor(stat[:, 2, s, :], vec[:, VEC["sinks"] + REP * g:VEC["sinks"] + REP * (g + 1)],
                                stat[:, 0, s, :], ALU.subtract).then_inc(max_steps, 1)

            def out_scale(s):
                dve.wait_ge(exp_done, s + 1)
                V.tensor_tensor(stat[:, 4, s, :], stat[:, 3, s, :], stat[:, 4, s, :], ALU.add).then_inc(den_steps, 1)
                dve.wait_ge(den_steps, 2 * s + 1)
                V.reciprocal(stat[:, 5, s, :], stat[:, 4, s, :]).then_inc(den_steps, 1)
                dve.wait_ge(den_steps, 2 * s + 2)
                dve.wait_ge(pv_done, s + 1)
                if s >= 2:
                    dve.wait_ge(oT_done, s - 1)
                V.tensor_tensor(oq[:, s % 2, :].rearrange("p (i d) -> p i d", i=REP),
                                bank[6][:, 0:REP * HD].rearrange("p (i d) -> p i d", i=REP),
                                stat[:, 5, s, :].rearrange("p (i o) -> p i o", o=1).broadcast_to([P, REP, HD]),
                                ALU.mult).then_inc(o_scaled, 1)

            def out_lo(s):
                n, g = s // KV, s % KV
                at = (slice(None), slice(2 * g, 2 * g + 2), slice(n * P, (n + 1) * P))
                dve.wait_ge(o_hi, s + 1)
                V.tensor_tensor(olo[at], bank[7][:, 0:2 * P].rearrange("p (j q) -> p j q", j=2),
                                ohi[at].bitcast(F32), ALU.subtract).then_inc(o_lo, 1)

            last = NBLK * KV - 1
            run(dve, qkv_step, 3, peel_first=True, peel_last=True)
            front(1)
            for s in range(last + 4):
                if 2 <= s <= last + 2:
                    out_scale(s - 2)
                if s >= 3:
                    out_lo(s - 3)
                if s + 2 <= last:
                    front(s + 2)
            finish("wo", "ffn1")

            feed_forward("ffn1", FF_PARTS, 1, "ain", 4)

            p = ph["ain"]
            dve.wait_ge(taps_split, 1)
            V.tensor_tensor(cwl[:], vec[:, VEC["conv_w"]:VEC["conv_w"] + C * TAPS], cwh[:].bitcast(F32),
                            ALU.subtract).then_inc(taps_split, 1)
            V.memset(hc[:, :, 0:TAPS - 1], 0.0).then_inc(hc_ready, 1)
            LATE_START = 2

            def own_taps(c):
                return range(PE_TAPS[c] + POOL_TAPS[c], TAPS - LATE_TAPS[c])

            def late_taps(c):
                return range(TAPS - LATE_TAPS[c], TAPS)

            def own_tap(c, n, k):
                x, w = hc[:, c % 2, k:k + T], v("conv_w", c * TAPS + k)
                if n == 0:
                    V.tensor_scalar(taps[:], x, w, None, ALU.mult).then_inc(tap_steps, 1)
                    return
                dve.wait_ge(tap_steps, sum(len(own_taps(j)) for j in range(c)) + n)
                V.scalar_tensor_tensor(hv[:, c, :] if n == len(own_taps(c)) - 1 else taps[:], x, w, taps[:],
                                       op0=ALU.mult, op1=ALU.add).then_inc(tap_steps, 1)

            def late_tap(c, n, k):
                x, w, at = hc[:, c % 2, k:k + T], v("conv_w", c * TAPS + k), bank[6 + c % 2][:]
                if n == 0:
                    dve.wait_ge(conv_done, c + 1)
                else:
                    dve.wait_ge(late_steps, sum(LATE_TAPS[:c]) + c + n)
                V.scalar_tensor_tensor(at, x, w, at, op0=ALU.mult, op1=ALU.add).then_inc(late_steps, 1)

            def collect(c):
                dve.wait_ge(tapped_steps, sum(POOL_TAPS[:c + 1]) - c - 1)
                dve.wait_ge(tap_steps, sum(len(own_taps(j)) for j in range(c + 1)))
                V.tensor_tensor(hv[:, c, :], prod[:, c % 2, :], hv[:, c, :], ALU.add).then_inc(late_steps, 1)
                dve.wait_ge(late_steps, sum(LATE_TAPS[:c + 1]) + c + 1)
                dve.wait_ge(conv_done, c + 1)
                V.tensor_tensor(hv[:, c, :], bank[6 + c % 2][:], hv[:, c, :], ALU.add).then_inc(hv_ready, 1)

            for c in range(C):
                b = c % 2
                if c == 0:
                    split_lo(p.unit, 0, AHEAD)
                    dve.wait_ge(norm_done, ND["ain"] + 2)
                    V.tensor_scalar(rinv[:], norm[0][:], EPS, None, ALU.mult).then_inc(rinv_ready, 1)
                    dve.wait_ge(rinv_ready, 5)
                    V.tensor_tensor(rinv[:], norm[1][:], rinv[:], ALU.add).then_inc(rinv_ready, 1)
                    V.memset(ssum[:], 0.0).then_inc(ssum_ready, 1)
                    dve.wait_ge(rms_ready, RR["ain"] + 1)
                    V.reciprocal(rinv[:], rms[:]).then_inc(rinv_ready, 1)
                    dve.wait_ge(rinv_ready, 7)
                for j in range(2):
                    k = 2 * b + j
                    dve.wait_ge(chain_done, p.chain + 2 * c + j + 1)
                    V.tensor_tensor(tmp[:, k, :], acc[k][:], rinv[:], ALU.mult).then_inc(acc_free, 1)
                if 0 < c < C - 1:
                    split_lo(p.unit, 0, 2 * c + AHEAD)
                dve.wait_ge(sig_ready, c + 1)
                if c >= 2:
                    dve.wait_ge(tapped_ready, sum(POOL_TAPS[:c - 1]))
                V.scalar_tensor_tensor(hc[:, b, TAPS - 1:TAPS - 1 + T], tmp[:, 2 * b, :], v("b_in", c),
                                       gate[:, b, :], op0=ALU.add, op1=ALU.mult).then_inc(hc_ready, 1)
                dve.wait_ge(hc_ready, c + 2)
                own, late = own_taps(c), late_taps(c - 1) if c else []
                for n in range(max(len(own), len(late) + LATE_START)):
                    if n < len(own):
                        own_tap(c, n, own[n])
                    if n == 2 and c < C - 1:
                        split_lo(p.unit, 0, 2 * c + 1 + AHEAD)
                    if n == (4 if 0 < c < C - 1 else 0):
                        dve.wait_ge(hch_ready, c + 1)
                        V.tensor_tensor(hcl[:, b, :], hc[:, b, :], hch[:, b, :].bitcast(F32), ALU.subtract)\
                            .then_inc(hcl_ready, 1)
                    if 0 <= n - LATE_START < len(late):
                        late_tap(c - 1, n - LATE_START, late[n - LATE_START])
                if c:
                    collect(c - 1)
            collect(C - 1)
            split_lo(p.unit, 0, 2 * C - 2 + AHEAD)
            dve.wait_ge(mean_done, 1)
            for c in range(C):
                V.scalar_tensor_tensor(hv[:, c, :], norm[0][:], -1.0 / D, hv[:, c, :],
                                       op0=ALU.mult, op1=ALU.add).then_inc(xc_ready, 1)
            for n, (c, e) in enumerate(((4, 5), (6, 7), (4, 6))):
                dve.wait_ge(xcsq_ready, 6 if n == 0 else C)
                if n == 2:
                    dve.wait_ge(late_sums, 2)
                V.tensor_tensor(square_of(c), square_of(c), square_of(e), ALU.add).then_inc(late_sums, 1)
            split_lo(p.unit, 0, 2 * C - 1 + AHEAD)
            dve.wait_ge(rms_ready, RR["mlp"])
            V.reciprocal(rinv[:], rms[:]).then_inc(rinv_ready, 1)
            dve.wait_ge(rinv_ready, 8)
            for c in range(C):
                V.tensor_tensor(hv[:, c, :], hv[:, c, :], rinv[:], ALU.mult).then_inc(ln_scaled, 1)
                if c >= 2:
                    dve.wait_ge(ln_hi, c - 1)
                    V.tensor_tensor(ylo[:, c - 2, :], hv[:, c - 2, :], yhi[:, c - 2, :].bitcast(F32),
                                    ALU.subtract).then_inc(ln_lo, 1)
            for c in (C - 2, C - 1):
                dve.wait_ge(ln_hi, c + 1)
                V.tensor_tensor(ylo[:, c, :], hv[:, c, :], yhi[:, c, :].bitcast(F32), ALU.subtract)\
                    .then_inc(ln_lo, 1)
            V.reciprocal(r1[:], r1[:]).then_inc(rinv_ready, 1)
            dve.wait_ge(rinv_ready, 9)
            finish("aout", "mlp", out_bias="b_out")

            feed_forward("mlp", MLP_PARTS, None, None, 10)


def _units(w):
    k, n = w.shape
    return np.ascontiguousarray(w.reshape(k // P, P, n // P, P).transpose(2, 1, 0, 3).reshape(n // P, P, k))


def _cols(v_):
    return v_.reshape(-1, P).T


def kernel(**inputs):
    import concourse.bacc as _bacc
    from concourse.bass_utils import run_bass_kernel_spmd as _run

    a = {k: np.asarray(t) for k, t in inputs.items()}
    w = {}
    w["pool"] = np.ascontiguousarray(
        a["pool_w"][0].reshape(4, 2, P, 2, P).transpose(0, 2, 3, 1, 4).reshape(4, P, 4 * P))
    for layer in range(2):
        wi = a["ffn_w_in"][layer].reshape(D, 2, FF_PAIRS, P).transpose(0, 2, 1, 3).reshape(D, -1)
        at = 0
        for q, n in enumerate(FF_PARTS):
            w[f"ffn{layer}_up{q}"] = _units(wi[:, 2 * at * P:2 * (at + n) * P])
            w[f"ffn{layer}_down{q}"] = _units(a["ffn_w_out"][layer][at * P:(at + n) * P])
            at += n
    heads = [8 * pr + REP * half + i for pr in range(2) for i in range(REP) for half in range(2)]
    nq = HEADS * HD

    def by_head(t):
        return t.reshape(t.shape[:-1] + (HEADS, HD))[..., heads, :].reshape(t.shape)

    wqkv, bqkv = a["attn_w_qkv"][0], a["attn_b_qkv"][0]
    w["qkv"] = _units(np.concatenate([by_head(wqkv[:, :nq]), wqkv[:, nq:]], axis=1))
    bq = np.concatenate([by_head(bqkv[:nq]), bqkv[nq:]])
    w["wo"] = _units(a["attn_w_o"][0])
    w["ain"] = _units(a["a_w_in_2"][0].reshape(D, 2, C, P).transpose(0, 2, 1, 3).reshape(D, -1))
    w["aout"] = _units(a["a_w_out_2"][0])
    at = 0
    for q, n in enumerate(MLP_PARTS):
        w[f"mlp_up{q}"] = _units(a["mlp_w1_2"][0][:, at * P:(at + n) * P])
        w[f"mlp_down{q}"] = _units(a["mlp_w2_2"][0][at * P:(at + n) * P])
        at += n

    glu = np.stack([*a["ffn_conv_w"].transpose(1, 0, 2), a["ffn_conv_b"]], axis=1)
    glu = glu.reshape(2, 4, 2, FF_PAIRS, P).transpose(4, 0, 3, 2, 1).reshape(P, -1)
    parts = {
        "pool_b": _cols(a["pool_b"][0].reshape(-1)), "pool_scale": _cols(a["pool_scale"][0]),
        "g_mix0": _cols(a["norm_mix"][0]), "g_mix1": _cols(a["norm_mix"][1]),
        "g_ffn0": _cols(a["norm_ffn"][0]), "g_ffn1": _cols(a["norm_ffn"][1]),
        "g_final": _cols(a["norm_f"]), "g_mix2": _cols(a["mix_norm_2"][0]), "g_mlp2": _cols(a["mlp_norm_2"][0]),
        "b_qkv": _cols(bq), "b_in": _cols(a["a_b_in_2"][0]), "conv_b": _cols(a["a_conv_b_2"][0]),
        "ln_g": _cols(a["a_ln_g_2"][0]), "ln_b": _cols(a["a_ln_b_2"][0]), "b_out": _cols(a["a_b_out_2"][0]),
        "sinks": np.broadcast_to(a["attn_sinks"][0], (P, HEADS)), "glu": glu,
        "conv_w": a["a_conv_w_2"][0].reshape(TAPS, C, P).transpose(2, 1, 0).reshape(P, -1),
    }
    vec = np.ascontiguousarray(np.concatenate([parts[name] for name, _ in VEC_PARTS], axis=1))

    dist = np.arange(P)[:, None] + P - np.arange(2 * P)[None, :]
    near = np.where((dist >= 0) & (dist < P), -dist, MASKED).astype(np.float32)
    inv = np.broadcast_to((1.0 / np.arange(1, PAD + 1)).astype(np.float32), (P, PAD))
    cst = np.ascontiguousarray(np.concatenate([near, inv, np.eye(P, dtype=np.float32)], axis=1))

    arrays = {"xT": np.ascontiguousarray(a["x"][0].T.reshape(C, P, T).transpose(1, 0, 2)), "vec_in": vec, "cst_in": cst}
    arrays.update({f"w_{k}": t for k, t in w.items()})
    nc = _bacc.Bacc("TRN2", target_bir_lowering=False, num_devices=1)
    aps = {k: nc.dram_tensor(k, t.shape, F32, kind="ExternalInput").ap() for k, t in arrays.items()}
    out = nc.dram_tensor("outT", (P, C, T), F32, kind="ExternalOutput").ap()
    build(nc, aps["xT"], aps["vec_in"], aps["cst_in"], {k: aps[f"w_{k}"] for k in w}, out)
    r = _run(nc, [arrays], core_ids=[0])
    y = r.results[0]["outT"]
    return np.ascontiguousarray(y.transpose(1, 0, 2).reshape(D, T).T)[None]
```
